# Optimizing a Trainium2 kernel written in Bass

```python
import jax, jax.numpy as jnp
from jax import lax
import numpy as np

D_MODEL = 1024
BATCH = 1
SEQ = 1024
DEPTH = 1

CHUNK = 64
Q_BLOCK = 128
N_MIXERS = 3
SB_HEADS = 16
SB_HEAD_DIM = D_MODEL // SB_HEADS
CONV_WIDTH = 3
ML_HEADS = 8
ML_QK_DIM = D_MODEL // (2 * ML_HEADS)
ML_V_DIM = D_MODEL // ML_HEADS
ML_QK_WIDTH = ML_HEADS * ML_QK_DIM
ML_IN_WIDTH = 2 * ML_QK_WIDTH + 2 * D_MODEL + 2 * ML_HEADS
D_FF = ((8 * D_MODEL + 3 * 256 - 1) // (3 * 256)) * 256
N_SB = (DEPTH + 2) // N_MIXERS
N_GC = (DEPTH + 1) // N_MIXERS
N_ML = DEPTH // N_MIXERS
RMS_EPS = 1e-6

kernel_name = "hybrid_stickbreak_conv_mlstm_encoder"

def rmsnorm(x, g):
    xf = x.astype(jnp.float32)
    y = xf * lax.rsqrt(jnp.mean(xf * xf, axis=-1, keepdims=True) + RMS_EPS)
    return (y * g.astype(jnp.float32)).astype(x.dtype)

def stick_breaking_mixer(h, w_qkv, w_o):
    bsz, seq, _ = h.shape
    q, k, v = jnp.split(h @ w_qkv, 3, axis=-1)

    def heads(t):
        return t.reshape(bsz, seq, SB_HEADS, SB_HEAD_DIM).transpose(0, 2, 1, 3)

    q, k, v = heads(q), heads(k), heads(v)
    scale = SB_HEAD_DIM ** -0.5
    outs = []
    for blk in range(seq // Q_BLOCK):
        t0, t1 = blk * Q_BLOCK, (blk + 1) * Q_BLOCK
        z = jnp.einsum('bhqd,bhkd->bhqk', q[:, :, t0:t1], k[:, :, :t1]).astype(jnp.float32) * scale
        before = jnp.arange(t1)[None, :] < jnp.arange(t0, t1)[:, None]
        log_stay = jnp.where(before, jax.nn.log_sigmoid(-z), 0.0)
        log_pass = lax.cumsum(log_stay, axis=3, reverse=True) - log_stay
        a = jnp.where(before, jnp.exp(jax.nn.log_sigmoid(z) + log_pass), 0.0)
        outs.append(jnp.einsum('bhqk,bhkd->bhqd', a.astype(v.dtype), v[:, :, :t1]))
    o = jnp.concatenate(outs, axis=2).transpose(0, 2, 1, 3).reshape(bsz, seq, D_MODEL)
    return o @ w_o

def gated_conv_mixer(h, w_in, conv_w, conv_b, w_out):
    b_gate, c_gate, u = jnp.split(h @ w_in, 3, axis=-1)
    cu = c_gate * u
    y = lax.conv_general_dilated(
        cu, conv_w[:, None, :].astype(cu.dtype), window_strides=(1,),
        padding=[(CONV_WIDTH - 1, 0)], dimension_numbers=('NWC', 'WIO', 'NWC'),
        feature_group_count=D_MODEL) + conv_b
    return (b_gate * y) @ w_out

def _mlstm_chunk_step(carry, inp):
    c_state, n_state, m_state = carry
    qc, kc, vc, igc, lfc = inp
    L = qc.shape[2]
    b = jnp.cumsum(lfc, axis=-1)
    causal = jnp.tril(jnp.ones((L, L), dtype=bool))
    log_d = jnp.where(causal, b[..., :, None] - b[..., None, :] + igc[..., None, :], -jnp.inf)
    m_inter = b + m_state[..., None]
    m_t = jnp.maximum(m_inter, jnp.max(log_d, axis=-1))
    d_mat = jnp.exp(log_d - m_t[..., None])
    inter = jnp.exp(m_inter - m_t)
    s = jnp.einsum('bhtd,bhsd->bhts', qc, kc) * d_mat
    num = jnp.einsum('bhts,bhsv->bhtv', s, vc) + inter[..., None] * jnp.einsum('bhvd,bhtd->bhtv', c_state, qc)
    den = jnp.sum(s, axis=-1) + inter * jnp.einsum('bhd,bhtd->bht', n_state, qc)
    h_out = num / jnp.maximum(jnp.abs(den), jnp.exp(-m_t))[..., None]
    b_last = b[..., -1]
    log_w = b_last[..., None] - b + igc
    m_new = jnp.maximum(b_last + m_state, jnp.max(log_w, axis=-1))
    w = jnp.exp(log_w - m_new[..., None])
    decay = jnp.exp(b_last + m_state - m_new)
    c_new = decay[..., None, None] * c_state + jnp.einsum('bhs,bhsv,bhsd->bhvd', w, vc, kc)
    n_new = decay[..., None] * n_state + jnp.einsum('bhs,bhsd->bhd', w, kc)
    return (c_new, n_new, m_new), h_out

def mlstm_mixer(h, w_in, b_i, b_f, w_out):
    bsz, seq, _ = h.shape
    cuts = [ML_QK_WIDTH, 2 * ML_QK_WIDTH, 2 * ML_QK_WIDTH + D_MODEL,
            2 * ML_QK_WIDTH + 2 * D_MODEL, 2 * ML_QK_WIDTH + 2 * D_MODEL + ML_HEADS]
    q, k, v, o_pre, i_pre, f_pre = jnp.split(h @ w_in, cuts, axis=-1)

    def heads(t, dh):
        return t.reshape(bsz, seq, ML_HEADS, dh).transpose(0, 2, 1, 3).astype(jnp.float32)

    q = heads(q, ML_QK_DIM)
    k = heads(k, ML_QK_DIM) * (ML_QK_DIM ** -0.5)
    v = heads(v, ML_V_DIM)
    ig = (i_pre + b_i).astype(jnp.float32).transpose(0, 2, 1)
    lf = jax.nn.log_sigmoid((f_pre + b_f).astype(jnp.float32)).transpose(0, 2, 1)
    n_chunks = seq // CHUNK

    def chunks(t):
        return jnp.moveaxis(t.reshape(bsz, ML_HEADS, n_chunks, CHUNK, *t.shape[3:]), 2, 0)

    init = (jnp.zeros((bsz, ML_HEADS, ML_V_DIM, ML_QK_DIM), jnp.float32),
            jnp.zeros((bsz, ML_HEADS, ML_QK_DIM), jnp.float32),
            jnp.zeros((bsz, ML_HEADS), jnp.float32))
    _, hs = lax.scan(_mlstm_chunk_step, init, (chunks(q), chunks(k), chunks(v), chunks(ig), chunks(lf)))
    hs = jnp.moveaxis(hs, 0, 2).reshape(bsz, ML_HEADS, seq, ML_V_DIM)
    hs = hs.transpose(0, 2, 1, 3).reshape(bsz, seq, D_MODEL).astype(h.dtype)
    return (jax.nn.sigmoid(o_pre) * hs) @ w_out

def swiglu_ffn(h, w_gu, w_down):
    g, u = jnp.split(h @ w_gu, 2, axis=-1)
    return (jax.nn.silu(g) * u) @ w_down

def setup_inputs(seed: int = 0) -> dict:
    key = jax.random.key(seed)
    ks = jax.random.split(key, 20)
    f32 = jnp.float32

    def dense(k, shape):
        return jax.random.normal(k, shape, f32) * (shape[-2] ** -0.5)

    def gain(k):
        return 1.0 + 0.05 * jax.random.normal(k, (DEPTH, D_MODEL), f32)

    return {
        "x": jax.random.normal(ks[0], (BATCH, SEQ, D_MODEL), f32),
        "ln_mix_pre": gain(ks[1]),
        "ln_mix_post": gain(ks[2]),
        "ln_ffn_pre": gain(ks[3]),
        "ln_ffn_post": gain(ks[4]),
        "sb_w_qkv": dense(ks[5], (N_SB, D_MODEL, 3 * D_MODEL)),
        "sb_w_o": dense(ks[6], (N_SB, D_MODEL, D_MODEL)),
        "gc_w_in": dense(ks[7], (N_GC, D_MODEL, 3 * D_MODEL)),
        "gc_conv_w": jax.random.normal(ks[8], (N_GC, CONV_WIDTH, D_MODEL), f32) * (CONV_WIDTH ** -0.5),
        "gc_conv_b": 0.02 * jax.random.normal(ks[9], (N_GC, D_MODEL), f32),
        "gc_w_out": dense(ks[10], (N_GC, D_MODEL, D_MODEL)),
        "ml_w_in": dense(ks[11], (N_ML, D_MODEL, ML_IN_WIDTH)),
        "ml_b_i": 0.1 * jax.random.normal(ks[12], (N_ML, ML_HEADS), f32),
        "ml_b_f": 3.0 + 0.5 * jax.random.normal(ks[13], (N_ML, ML_HEADS), f32),
        "ml_w_out": dense(ks[14], (N_ML, D_MODEL, D_MODEL)),
        "ffn_w_gu": dense(ks[15], (DEPTH, D_MODEL, 2 * D_FF)),
        "ffn_w_down": dense(ks[16], (DEPTH, D_FF, D_MODEL)),
    }

def reference(x, ln_mix_pre, ln_mix_post, ln_ffn_pre, ln_ffn_post,
              sb_w_qkv, sb_w_o, gc_w_in, gc_conv_w, gc_conv_b, gc_w_out,
              ml_w_in, ml_b_i, ml_b_f, ml_w_out, ffn_w_gu, ffn_w_down):
    for i in range(DEPTH):
        kind, j = i % N_MIXERS, i // N_MIXERS
        hn = rmsnorm(x, ln_mix_pre[i])
        if kind == 0:
            mixed = stick_breaking_mixer(hn, sb_w_qkv[j], sb_w_o[j])
        elif kind == 1:
            mixed = gated_conv_mixer(hn, gc_w_in[j], gc_conv_w[j], gc_conv_b[j], gc_w_out[j])
        else:
            mixed = mlstm_mixer(hn, ml_w_in[j], ml_b_i[j], ml_b_f[j], ml_w_out[j])
        x = x + rmsnorm(mixed, ln_mix_post[i])
        hn = rmsnorm(x, ln_ffn_pre[i])
        x = x + rmsnorm(swiglu_ffn(hn, ffn_w_gu[i], ffn_w_down[i]), ln_ffn_post[i])
    return x


_drawn_inputs = setup_inputs


def setup_inputs(seed=0):
    import zlib

    import numpy as np

    out = dict(_drawn_inputs(seed))
    spreads = {}
    factors = {}
    for name, (base, spread) in spreads.items():
        noise = np.random.default_rng([zlib.crc32(name.encode()), seed]).standard_normal(out[name].shape)
        drawn = base * np.exp(spread * noise) if base else spread * noise
        out[name] = __import__('jax').numpy.asarray(drawn.astype(out[name].dtype))
    for name, factor in factors.items():
        out[name] = (out[name] * factor).astype(out[name].dtype)
    return out
```

```python
from contextlib import ExitStack

import concourse.bass as bass
from concourse import mybir

F32 = mybir.dt.float32
F32R = mybir.dt.float32r
ALU = mybir.AluOpType
ACT = mybir.ActivationFunctionType

P = 128
D = 1024
SEQ = 1024
KT = D // P
NT = SEQ // P
HALF = 512
HD = 64
PAIRS = D // (2 * HD)
D_FF = ((8 * D + 3 * 256 - 1) // (3 * 256)) * 256
NF = D_FF // P
NG = NF // 2
Z_SCALE = HD ** -0.5
EPS = 1e-6
UNITS1 = 4 * PAIRS
UNITS = UNITS1 + 3 * NF
SLOTS = 32

ROW_W = [SEQ - P * r for r in range(NT)]
ROW_AT = [sum(ROW_W[:r]) if r < 4 else sum(ROW_W[4:r]) for r in range(NT)]
A_SIZE = [sum(ROW_W[:4]), sum(ROW_W[4:])]


def row_chunks(r):
    return [(P * r, HALF), (HALF, SEQ)] if r < 4 else [(P * r, SEQ)]


CHUNKS = [(r, a, b, n == len(row_chunks(r)) - 1) for r in range(NT) for n, (a, b) in enumerate(row_chunks(r))]
NCH = len(CHUNKS)
LAST_CHUNK = [max(n for n, c in enumerate(CHUNKS) if c[0] == r) for r in range(NT)]

Z_SLOT = {16 * h + c: (h, c) for h in range(2) for c in range(NCH)}
ROW_SLOT = {16 * h + LAST_CHUNK[r] + 1: (h, r) for h in range(2) for r in range(NT)}
T_SLOT = {}
for _n, _s in enumerate((0, 1, 2, 3)):
    T_SLOT[_s] = (_n, "prev", 1, 4 + _n)
for _n, _s in enumerate((6, 7)):
    T_SLOT[_s] = (4 + _n, "v", 0, 4 * _n)
for _n in range(8):
    T_SLOT[8 + _n] = (6 + _n, "lo", 0, _n)
    T_SLOT[24 + _n] = (18 + _n, "lo", 1, _n)
for _n, _s in enumerate((16, 18, 20, 22)):
    T_SLOT[_s] = (14 + _n, "up", 0, 4 + _n)
T_PER_STEP = 26
T_START = 2 * NT
AV_LAG = 2


def t_index(p, n):
    return T_START - 4 + T_PER_STEP * p + n


def av_index(p, kind, h, j):
    if kind == "prev":
        return 2 * NCH * p - 4 + (j - 4)
    return 2 * NCH * p + NCH * h + (j if kind == "lo" else 8 + j - 4)


def t_of_av(p, kind, h, j):
    n = next(v[0] for v in T_SLOT.values() if v[1:] == (kind, h, j))
    return t_index(p, n)


def acc_base(p):
    return 6 if isinstance(p, int) and p == 0 else 12 + 22 * (p - 1)


def unit_base(p):
    return 3 if isinstance(p, int) and p == 0 else 6 + 4 * (p - 1)


ACC_OFF = {"q": 0, "wo": 2, "k": 18, "v": 20}
UNIT_OFF = {"q": 0, "wo": 1, "k": 2, "v": 3}


def step_units(p, kind):
    if isinstance(p, int) and p == 0:
        n = {"q": 0, "k": 1, "v": 2}[kind]
        return 6 + 2 * n, 3 + n
    if isinstance(p, int) and p >= PAIRS - 1:
        return acc_base(PAIRS - 1) + 16 * (p - (PAIRS - 1)), unit_base(PAIRS - 1) + p - (PAIRS - 1)
    return acc_base(p) + ACC_OFF[kind], unit_base(p) + UNIT_OFF[kind]


def unit_slot(p, kind):
    if isinstance(p, int):
        return step_units(p, kind)[1] % 2
    return UNIT_OFF[kind] % 2


ACC_END = 12 + 22 * (PAIRS - 2) + 32
T_TRANS = T_START - 4 + T_PER_STEP * PAIRS + 4
T_END = T_TRANS + 2 * NT
FILL_KIND = ["q", "wo", "k", "v"]


def encoder_layer(nc, x, g_mix_pre, g_mix_post, g_ffn_pre, g_ffn_post, units, out):
    ctx = ExitStack()
    with ctx:
        def sem(name):
            return ctx.enter_context(nc.semaphore(name))

        def alloc(stack, name, shape, dt=F32):
            return stack.enter_context(nc.sbuf_tensor(name, shape, dt))

        hnT_hi = alloc(ctx, "hnT_hi", [P, KT, SEQ], F32R)
        hnT_lo = alloc(ctx, "hnT_lo", [P, KT, SEQ], F32R)
        acc = alloc(ctx, "acc", [P, NT, D])
        raw = alloc(ctx, "raw", [P, 2, D])
        w_hi01 = alloc(ctx, "w_hi01", [P, 2, D], F32R)
        w_lo01 = alloc(ctx, "w_lo01", [P, 2, D], F32R)
        ident = alloc(ctx, "ident", [P, P])
        keep = alloc(ctx, "keep", [P, P], mybir.dt.bfloat16)
        ss = alloc(ctx, "ss", [P, 4 * NT])
        ms = alloc(ctx, "ms", [P, 3 * NT])
        rstd = alloc(ctx, "rstd", [P, 3 * NT])
        mhalf = alloc(ctx, "mhalf", [P, 1])

        with ExitStack() as one:
            A = [alloc(one, f"A{n}", [P, A_SIZE[n]]) for n in range(2)]
            with ExitStack() as qk:
                q_hi = alloc(qk, "q_hi", [P, 2, SEQ], F32R)
                q_lo = alloc(qk, "q_lo", [P, 2, SEQ], F32R)
                k_hi = alloc(qk, "k_hi", [P, 2, SEQ], F32R)
                k_lo = alloc(qk, "k_lo", [P, 2, SEQ], F32R)
                V = alloc(qk, "V", [P, NT, 2, 2, HD], F32R)
                vT = alloc(qk, "vT", [P, SEQ])
                stay = [alloc(qk, "stay0", [P, 1 + SEQ]), alloc(qk, "stay1", [P, 1 + SEQ - P])]
                AT_hi = alloc(qk, "AT_hi", [P, 2, HALF], F32R)
                AT_lo = alloc(qk, "AT_lo", [P, 2, HALF], F32R)
                oT_hi = alloc(qk, "oT_hi", [P, SEQ], F32R)
                oT_lo = alloc(qk, "oT_lo", [P, SEQ], F32R)
                o_part = alloc(qk, "o_part", [P, HALF // 2])
            with ExitStack() as tr:
                g_post_t = alloc(tr, "g_post_t", [P, D])
                g_ffn_t = alloc(tr, "g_ffn_t", [P, D])
                x_in = alloc(tr, "x_in", [P, 2, D])
                hn_t = alloc(tr, "hn_t", [P, 2, D])
                junk_t = alloc(tr, "junk_t", [P, D])
        with ExitStack() as st:
            g_pre_s = alloc(st, "g_pre_s", [P, D])
            hn_s = alloc(st, "hn_s", [P, 2, D])
            junk_s = alloc(st, "junk_s", [P, D])
        with ExitStack() as two:
            w_hi2 = alloc(two, "w_hi2", [P, D], F32R)
            w_lo2 = alloc(two, "w_lo2", [P, D], F32R)
            g_out = alloc(two, "g_out", [P, D])
            sg = alloc(two, "sg", [P, 2, HALF])
            alloc(two, "gap", [P, sum(A_SIZE) - 4 * D])
            y = alloc(two, "y", [P, NT, D])
            h_hi = alloc(two, "h_hi", [P, 2, 2, SEQ], F32R)
            h_lo = alloc(two, "h_lo", [P, 2, 2, SEQ], F32R)

        bank = [ctx.enter_context(nc.psum_tensor(f"bank{n}", [P, HALF], F32)) for n in range(8)]
        ACCB = bank[0:2]
        ZB = bank[2:4]
        TB = bank[4:6]
        OB = bank[6:8]
        GATEB, UPB = ZB, OB
        YB = ACCB + TB

        w_hi = [w_hi01[:, 0, :], w_hi01[:, 1, :], w_hi2[:, :]]
        w_lo = [w_lo01[:, 0, :], w_lo01[:, 1, :], w_lo2[:, :]]

        x_tile = [sem(f"x_tile{t}") for t in range(NT)]
        raw_in = [sem("raw_in0"), sem("raw_in1")]
        gain_in = sem("gain_in")
        gain2_in = sem("gain2_in")
        gain3_in = sem("gain3_in")
        x_again = [sem("x_again0"), sem("x_again1")]
        out_done = sem("out_done")
        consts = sem("consts")
        w_hi_ready = sem("w_hi_ready")
        w_ready = sem("w_ready")
        sq_done = sem("sq_done")
        ms_done = sem("ms_done")
        rstd_done = sem("rstd_done")
        hn_ready = sem("hn_ready")
        mix_scaled = sem("mix_scaled")
        x2_ready = sem("x2_ready")
        t_full = sem("t_full")
        t_hi = sem("t_hi")
        t_lo = sem("t_lo")
        acc_full = sem("acc_full")
        acc_hi = sem("acc_hi")
        acc_free = sem("acc_free")
        z_full = sem("z_full")
        sig_done = sem("sig_done")
        mask_done = sem("mask_done")
        scan_done = sem("scan_done")
        row_done = sem("row_done")
        av_done = sem("av_done")
        o_half = sem("o_half")
        o_sum = sem("o_sum")
        o_lo = sem("o_lo")
        gate_full = sem("gate_full")
        up_full = sem("up_full")
        sg_ready = sem("sg_ready")
        silu_ready = sem("silu_ready")
        prod_ready = sem("prod_ready")
        h_hi_ready = sem("h_hi_ready")
        h_ready = sem("h_ready")
        y_zero = sem("y_zero")
        y_full = sem("y_full")
        y_free = sem("y_free")
        ysq_done = sem("ysq_done")
        y_scaled = sem("y_scaled")
        out_ready = sem("out_ready")

        x_tiles = x.rearrange("b (t p) d -> p (b t) d", p=P)
        out_tiles = out.rearrange("b (t p) d -> p (b t) d", p=P)

        block = ctx.enter_context(nc.Block())

        def before_count(p, kind):
            return step_units(p, kind)[0]

        @block.sync
        def _(sp):
            for t in range(4):
                sp.dma_start(acc[:, t, :], x_tiles[:, t, :]).then_inc(x_tile[t], 16)
            sp.dma_start(raw[:, 0, :], units[0]).then_inc(raw_in[0], 16)
            for t in range(4, NT):
                sp.dma_start(acc[:, t, :], x_tiles[:, t, :]).then_inc(x_tile[t], 16)
            sp.dma_start(raw[:, 1, :], units[1]).then_inc(raw_in[1], 16)
            with sp.Fori(1, UNITS // 2) as i:
                for s in range(2):
                    sp.wait_ge(w_ready, 2 * i + s - 1)
                    sp.dma_start(raw[:, s, :], units[bass.ds(2 * i + s, 1)].rearrange("a p n -> p (a n)")
                                 ).then_inc(raw_in[s], 16)
            for t in range(NT):
                sp.wait_ge(out_ready, t + 1)
                sp.dma_start(out_tiles[:, t, :], y[:, t, :]).then_inc(out_done, 16)
            sp.wait_ge(out_done, 16 * NT)

        @block.scalar
        def _(act):
            def split_hi(n, slot, raw_slot, count):
                act.wait_ge(raw_in[raw_slot], count)
                nc.scalar.activation(w_hi[slot], raw[:, raw_slot, :], ACT.Copy).then_inc(w_hi_ready, 1)

            def raw_count(n, parity):
                return 16 * (n // 2 + 1) if isinstance(n, int) else 8 * (n - parity) + 16

            def t_hi_copy(index, par, out_ap, in_ap):
                act.wait_ge(t_full, index + 1)
                nc.scalar.activation(out_ap, in_ap, ACT.Copy).then_inc(t_hi, 1)

            act.dma_start(g_pre_s[:, :], g_mix_pre.partition_broadcast(P)).then_inc(gain_in, 16)

            def start_hi(t):
                for half in range(2):
                    n = 2 * t + half
                    t_hi_copy(n, n % 2, hnT_hi[:, 4 * half:4 * half + 4, t * P:(t + 1) * P],
                              TB[n % 2][:, :].rearrange("p (k c) -> p k c", k=4))

            for t in range(NT):
                act.wait_ge(x_tile[t], 16)
                if t:
                    act.wait_ge(sq_done, t)
                nc.scalar.activation(junk_s[:, :], acc[:, t, :], ACT.Square,
                                     accum_out=ss[:, t:t + 1]).then_inc(sq_done, 1)
                if t == 1:
                    split_hi(0, 0, 0, 16)
                    split_hi(1, 1, 1, 16)
                if t >= 2:
                    start_hi(t - 2)
            start_hi(NT - 2)
            start_hi(NT - 1)

            def qk_hi(index, kind, par, c):
                act.wait_ge(acc_full, index + 1)
                dst = q_hi if kind == "q" else k_hi
                nc.scalar.activation(dst[:, par, c * HALF:(c + 1) * HALF], ACCB[c][:, :],
                                     ACT.Copy).then_inc(acc_hi, 1)

            for n, kind in enumerate("qkv"):
                if n:
                    act.wait_ge(acc_full, 2 * n)
                    split_hi(n + 1, (n + 1) % 2, (n + 1) % 2, raw_count(n + 1, 0))
                for c in range(2):
                    if kind != "v":
                        qk_hi(2 * n + c, kind, 0, c)

            def split_slot(p, s):
                st = s // 8
                kind = FILL_KIND[st]
                if isinstance(p, int) and p == 0:
                    if kind == "wo":
                        return
                    n = {"q": 4, "k": 5, "v": 6}[kind]
                    act.wait_ge(acc_full, before_count(p, kind))
                    split_hi(n, n % 2, n % 2, raw_count(n, 0))
                elif isinstance(p, int) and p == PAIRS - 1:
                    if kind == "wo":
                        act.wait_ge(acc_full, before_count(p, kind))
                        split_hi(31, 1, 1, raw_count(31, 1))
                else:
                    n = unit_base(p) + UNIT_OFF[kind] + 1
                    par = (UNIT_OFF[kind] + 1) % 2
                    act.wait_ge(acc_full, before_count(p, kind))
                    split_hi(n, par, par, raw_count(n, par))

            def o_copy(p, h, half_q, half):
                sb = 4 * p + 2 * h + half_q
                act.wait_ge(av_done, 2 * NCH * p + NCH * h + (NCH if half_q else 8))
                if not (isinstance(sb, int) and sb == 0 and half == 0):
                    act.wait_ge(o_lo, 2 * sb + half)
                rows = slice(HD * h, HD * (h + 1))
                nc.scalar.activation(o_part[rows, :], OB[half_q][HD:P, half * 256:half * 256 + 256],
                                     ACT.Copy).then_inc(o_half, 1)

            O_SLOT = {2: (-1, 1, 0, 0), 3: (-1, 1, 0, 1), 6: (-1, 1, 1, 0), 7: (-1, 1, 1, 1),
                      18: (0, 0, 0, 0), 19: (0, 0, 0, 1), 25: (0, 0, 1, 0), 26: (0, 0, 1, 1)}

            def step(p, par, first=False, proj=True, wo=True, slots=SLOTS):
                for s in range(slots):
                    tail = slots < SLOTS
                    if s in T_SLOT:
                        n, kind, h, j = T_SLOT[s]
                        g = t_index(p, n)
                        b = n % 2
                        if kind == "v" and not tail:
                            if not first:
                                act.wait_ge(av_done, 2 * NCH * p)
                            t_hi_copy(g, b, V[:, j:j + 4, :, 0, :],
                                      TB[b][:, :].rearrange("p (k h c) -> p k h c", k=4, h=2))
                        elif kind != "v" and not (kind == "prev" and first):
                            a = av_index(p, kind, h, j)
                            if not (isinstance(a, int) and a < 2):
                                act.wait_ge(av_done, a - 1)
                            w = P * (min(j, 3) + 1 if kind == "lo" else j - 3)
                            t_hi_copy(g, b, AT_hi[:, b, 0:w], TB[b][:, 0:w])
                    if s in Z_SLOT and not tail:
                        h, c = Z_SLOT[s]
                        r, a, e, _ = CHUNKS[c]
                        z = 2 * NCH * p + NCH * h + c
                        R = 16 * p + 8 * h + r
                        if (c == 0 or CHUNKS[c - 1][0] != r) and not (isinstance(R, int) and R < 2):
                            act.wait_ge(row_done, R - 1)
                        act.wait_ge(z_full, z + 1)
                        at = ROW_AT[r] + a - P * r
                        nc.scalar.activation(A[r // 4][:, at:at + e - a], ZB[c % 2][:, 0:e - a],
                                             ACT.Sigmoid, scale=Z_SCALE)
                        nc.scalar.activation(stay[r % 2][:, 1 + a - P * r:1 + e - P * r], ZB[c % 2][:, 0:e - a],
                                             ACT.Sigmoid, scale=-Z_SCALE).then_inc(sig_done, 1)
                    if proj and s in (4, 8, 20, 24) and not tail:
                        kind = "q" if s < 16 else "k"
                        c = 0 if s % 8 == 4 else 1
                        qk_hi(step_units(p, kind)[0] + c, kind, 1 - par, c)
                    if s in O_SLOT and not (first and O_SLOT[s][0] < 0):
                        dp, h, half_q, half = O_SLOT[s]
                        o_copy(p + dp, h, half_q, half)
                    if s % 8 == 1 and not tail:
                        split_slot(p, s)

            step(0, 0, first=True, wo=False)
            with act.Fori(0, PAIRS // 2 - 1) as i:
                for u in range(2):
                    step(2 * i + 1 + u, (1 + u) % 2)
            step(PAIRS - 1, 1, proj=False)

            act.wait_ge(z_full, 2 * NCH * PAIRS)
            act.dma_start(g_post_t[:, :], g_mix_post.partition_broadcast(P)).then_inc(gain2_in, 16)
            act.dma_start(g_ffn_t[:, :], g_ffn_pre.partition_broadcast(P)).then_inc(gain2_in, 16)
            for t in range(2):
                act.dma_start(x_in[:, t, :], x_tiles[:, t, :]).then_inc(x_again[t], 16)
            step(PAIRS, 0, proj=False, slots=8)

            def split_at(m, waits):
                for s, v in waits:
                    act.wait_ge(s, v)
                split_hi(UNITS1 + m, m % 3, m % 2, 16 * ((UNITS1 + m) // 2 + 1))

            def square(src, index):
                if index != NT:
                    act.wait_ge(sq_done, index)
                nc.scalar.activation(junk_t[:, :], src, ACT.Square,
                                     accum_out=ss[:, index:index + 1]).then_inc(sq_done, 1)

            split_at(0, [(acc_full, ACC_END - 16)])
            for k in range(NT + 3):
                if k < NT:
                    act.wait_ge(acc_free, ACC_END - 16 + 2 * (k + 1))
                    nsq = NT + (2 * k - 1 if k else 0)
                    act.wait_ge(sq_done, nsq)
                    nc.scalar.activation(junk_t[:, :], acc[:, k, :], ACT.Square,
                                         accum_out=ss[:, NT + k:NT + k + 1]).then_inc(sq_done, 1)
                if 1 <= k <= NT:
                    act.wait_ge(x2_ready, k)
                    if k + 1 < NT:
                        act.dma_start(x_in[:, (k + 1) % 2, :], x_tiles[:, k + 1, :]
                                      ).then_inc(x_again[(k + 1) % 2], 16)
                    nsq = NT + 2 * k if k < NT else 3 * NT - 1
                    act.wait_ge(sq_done, nsq)
                    nc.scalar.activation(junk_t[:, :], acc[:, k - 1, :], ACT.Square,
                                         accum_out=ss[:, 2 * NT + k - 1:2 * NT + k]).then_inc(sq_done, 1)
                if k >= 3:
                    t = k - 3
                    for half in range(2):
                        n = T_TRANS + 2 * t + half
                        t_hi_copy(n, n % 2, hnT_hi[:, 4 * half:4 * half + 4, t * P:(t + 1) * P],
                                  TB[n % 2][:, :].rearrange("p (k c) -> p k c", k=4))
            act.dma_start(g_out[:, :], g_ffn_post.partition_broadcast(P)).then_inc(gain3_in, 16)

            def ffn_chunk(g, e, par, c):
                n = 4 * g + 2 * e + c
                act.wait_ge(up_full, n + 1)
                if not (isinstance(n, int) and n < 2):
                    act.wait_ge(h_ready, n - 1)
                nc.scalar.activation(sg[:, c, :], GATEB[c][:, :], ACT.Sigmoid).then_inc(sg_ready, 1)
                act.wait_ge(prod_ready, n + 1)
                nc.scalar.activation(h_hi[:, par, e, c * HALF:(c + 1) * HALF], sg[:, c, :],
                                     ACT.Copy).then_inc(h_hi_ready, 1)

            split_at(1, [(acc_full, ACC_END)])
            split_at(2, [])
            split_at(3, [(gate_full, 2)])
            for c in range(2):
                ffn_chunk(0, 0, 0, c)
            split_at(4, [(up_full, 2)])
            split_at_5 = [(gate_full, 4)]
            for c in range(2):
                ffn_chunk(0, 1, 0, c)

            def ffn_step(g, par, m_mod):
                base = 6 * g - 2

                def split(off, s, count):
                    act.wait_ge(s, count)
                    n = UNITS1 + base + off
                    rp = off % 2
                    rc = 16 * (n // 2 + 1) if isinstance(n, int) else 8 * (n - rp) + 16
                    split_hi(n, (m_mod + off) % 3, rp, rc)

                split(1, gate_full, 4 * g + 1)
                split(2, gate_full, 4 * g + 1)
                split(3, gate_full, 4 * g + 2)
                ffn_chunk(g, 0, par, 0)
                split(4, up_full, 4 * g + 2)
                ffn_chunk(g, 0, par, 1)
                split(5, gate_full, 4 * g + 4)
                ffn_chunk(g, 1, par, 0)
                split(6, up_full, 4 * g + 4)
                ffn_chunk(g, 1, par, 1)

            with act.Fori(0, (NG - 1) // 2) as i:
                for u in range(2):
                    ffn_step(2 * i + 1 + u, (1 + u) % 2, (4 + 6 * u) % 3)
            act.wait_ge(y_full, 16 * (NG - 1))
            m = 6 * (NG - 1) + 5
            split_hi(UNITS1 + m, m % 3, m % 2, 16 * ((UNITS1 + m) // 2 + 1))
            for t in range(NT):
                act.wait_ge(y_free, 16 * (NG - 1) + 2 * t + 2)
                for c in range(2):
                    if t or c:
                        act.wait_ge(ysq_done, 2 * t + c)
                    nc.scalar.activation(sg[:, c, :], y[:, t, c * HALF:(c + 1) * HALF], ACT.Square,
                                         accum_out=ss[:, (2 * t + c):(2 * t + c) + 1]).then_inc(ysq_done, 1)

        @block.gpsimd
        def _(pool):
            nc.gpsimd.memset(ident[:, :], 0.0).then_inc(consts, 1)
            nc.gpsimd.memset(mhalf[:, :], -0.5).then_inc(consts, 1)
            for b in range(2):
                nc.gpsimd.memset(stay[b][:, 0:1], 1.0).then_inc(consts, 1)
            nc.gpsimd.memset(keep[:, :], 1.0).then_inc(consts, 1)
            pool.wait_ge(consts, 5)
            nc.gpsimd.affine_select(out=ident[:, :], in_=ident[:, :], compare_op=ALU.not_equal, fill=1.0,
                                    base=0, pattern=[[-1, P]], channel_multiplier=1).then_inc(consts, 1)
            nc.gpsimd.affine_select(out=keep[:, :], in_=keep[:, :], compare_op=ALU.is_gt, fill=0.0,
                                    base=0, pattern=[[1, P]], channel_multiplier=-1).then_inc(consts, 1)
            pool.wait_ge(consts, 7)

            def split_lo(n, slot, raw_slot):
                pool.wait_ge(w_hi_ready, n + 1)
                nc.gpsimd.tensor_tensor(w_lo[slot], raw[:, raw_slot, :], w_hi[slot].bitcast(F32),
                                        ALU.subtract).then_inc(w_ready, 1)

            def inverse_rms(col, count):
                nc.gpsimd.tensor_scalar(ms[:, col:col + 1], ss[:, col:col + 1], 1.0 / D, EPS,
                                        ALU.mult, ALU.add).then_inc(ms_done, 1)
                pool.wait_ge(ms_done, count + 1)
                nc.gpsimd.tensor_tensor(rstd[:, col:col + 1], ms[:, col:col + 1], mhalf[:, :],
                                        ALU.pow).then_inc(rstd_done, 1)

            for t in range(NT):
                pool.wait_ge(sq_done, t + 1)
                inverse_rms(t, t)
                if t == 2:
                    split_lo(0, 0, 0)
                if t == 5:
                    split_lo(1, 1, 1)
            split_lo(2, 0, 0)
            split_lo(3, 1, 1)

            def step(p, par, first=False, proj=True, slots=SLOTS):
                tail = slots < SLOTS
                for s in range(slots):
                    if s in Z_SLOT and not tail:
                        h, c = Z_SLOT[s]
                        r, a, _, _ = CHUNKS[c]
                        if a == P * r:
                            pool.wait_ge(sig_done, 2 * NCH * p + NCH * h + c + 1)
                            diag = A[r // 4][:, ROW_AT[r]:ROW_AT[r] + P]
                            nc.gpsimd.tensor_tensor(diag, diag, keep[:, :], ALU.mult)
                            diag = stay[r % 2][:, 1:1 + P]
                            nc.gpsimd.affine_select(out=diag, in_=diag, compare_op=ALU.is_gt, fill=1.0, base=0,
                                                    pattern=[[1, P]], channel_multiplier=-1).then_inc(mask_done, 1)
                    if s % 8 == 1 and not tail:
                        kind = FILL_KIND[s // 8]
                        if isinstance(p, int) and p == 0:
                            if kind != "wo":
                                n = {"q": 4, "k": 5, "v": 6}[kind]
                                split_lo(n, n % 2, n % 2)
                        elif isinstance(p, int) and p == PAIRS - 1:
                            if kind == "wo":
                                split_lo(31, 1, 1)
                        else:
                            q = (UNIT_OFF[kind] + 1) % 2
                            split_lo(unit_base(p) + UNIT_OFF[kind] + 1, q, q)

            step(0, 0, first=True)
            with pool.Fori(0, PAIRS // 2 - 1) as i:
                for u in range(2):
                    step(2 * i + 1 + u, (1 + u) % 2)
            step(PAIRS - 1, 1, proj=False)
            step(PAIRS, 0, slots=8)

            split_lo(UNITS1, 0, 0)
            for k in range(NT + 2):
                if k < NT:
                    pool.wait_ge(sq_done, NT + (2 * k if k else 0) + (1 if k == 0 else 0))
                    inverse_rms(NT + k, NT + (2 * k - 1 if k else 0))
                if 1 <= k <= NT:
                    t = k - 1
                    pool.wait_ge(mix_scaled, t + 1)
                    pool.wait_ge(x_again[t % 2], 16 * (t // 2 + 1))
                    nc.gpsimd.tensor_tensor(acc[:, t, :], acc[:, t, :], x_in[:, t % 2, :],
                                            ALU.add).then_inc(x2_ready, 1)
                    pool.wait_ge(sq_done, NT + 2 * k + 1 if k < NT else 3 * NT)
                    inverse_rms(2 * NT + t, NT + 2 * k if k < NT else 3 * NT - 1)
            split_lo(UNITS1 + 1, 1, 1)
            split_lo(UNITS1 + 2, 2, 0)
            split_lo(UNITS1 + 3, 0, 1)
            pool.wait_ge(hn_ready, 2 * NT)
            pool.wait_ge(t_lo, T_END)
            nc.gpsimd.memset(y[:, :, :], 0.0).then_inc(y_zero, 1)

            def h_lo_chunk(g, e, par, c):
                n = 4 * g + 2 * e + c
                pool.wait_ge(h_hi_ready, n + 1)
                cols = slice(c * HALF, (c + 1) * HALF)
                nc.gpsimd.tensor_tensor(h_lo[:, par, e, cols], sg[:, c, :], h_hi[:, par, e, cols].bitcast(F32),
                                        ALU.subtract).then_inc(h_ready, 1)

            for c in range(2):
                h_lo_chunk(0, 0, 0, c)
            split_lo(UNITS1 + 4, 1, 0)
            for c in range(2):
                h_lo_chunk(0, 1, 0, c)
            with pool.Fori(0, (NG - 1) // 2) as i:
                for u in range(2):
                    g, par, m_mod = 2 * i + 1 + u, (1 + u) % 2, (4 + 6 * u) % 3
                    base = UNITS1 + 6 * g - 2
                    for off in (1, 2, 3):
                        split_lo(base + off, (m_mod + off) % 3, off % 2)
                    for off in (4, 5, 6, None):
                        e, c = (0, 0) if off == 4 else (0, 1) if off == 5 else (1, 0) if off == 6 else (1, 1)
                        h_lo_chunk(g, e, par, c)
                        if off:
                            split_lo(base + off, (m_mod + off) % 3, off % 2)
            m = 6 * (NG - 1) + 5
            split_lo(UNITS1 + m, m % 3, m % 2)
            for t in range(NT):
                pool.wait_ge(ysq_done, 2 * t + 2)
                nc.gpsimd.tensor_tensor(ss[:, 3 * NT + t:3 * NT + t + 1], ss[:, 2 * t:2 * t + 1],
                                        ss[:, 2 * t + 1:2 * t + 2], ALU.add).then_inc(ms_done, 1)
                pool.wait_ge(ms_done, 3 * NT + 2 * t + 1)
                nc.gpsimd.tensor_scalar(ms[:, t:t + 1], ss[:, 3 * NT + t:3 * NT + t + 1], 1.0 / D, EPS,
                                        ALU.mult, ALU.add).then_inc(ms_done, 1)
                pool.wait_ge(ms_done, 3 * NT + 2 * t + 2)
                nc.gpsimd.tensor_tensor(rstd[:, t:t + 1], ms[:, t:t + 1], mhalf[:, :],
                                        ALU.pow).then_inc(rstd_done, 1)

        @block.vector
        def _(dve):
            def t_lo_sub(index, out_ap, in_ap, hi_ap):
                dve.wait_ge(t_hi, index + 1)
                nc.vector.tensor_tensor(out_ap, in_ap, hi_ap.bitcast(F32), ALU.subtract).then_inc(t_lo, 1)

            def norm_lo(index, t, half):
                ks, cols = slice(4 * half, 4 * half + 4), slice(t * P, (t + 1) * P)
                t_lo_sub(index, hnT_lo[:, ks, cols], TB[index % 2][:, :].rearrange("p (k c) -> p k c", k=4),
                         hnT_hi[:, ks, cols])

            dve.wait_ge(gain_in, 16)
            for t in range(NT + 1):
                if t < NT:
                    dve.wait_ge(rstd_done, t + 1)
                    if t >= 2:
                        dve.wait_ge(t_full, 2 * (t - 1))
                    nc.vector.scalar_tensor_tensor(out=hn_s[:, t % 2, :], in0=acc[:, t, :],
                                                   scalar=rstd[:, t:t + 1], in1=g_pre_s[:, :],
                                                   op0=ALU.mult, op1=ALU.mult).then_inc(hn_ready, 1)
                if t:
                    norm_lo(2 * t - 2, t - 1, 0)
                    norm_lo(2 * t - 1, t - 1, 1)
            dve.wait_ge(hn_ready, NT)
            for t in range(NT):
                nc.vector.memset(acc[:, t, :], 0.0)

            def qk_lo(index, hi_count, kind, par, c):
                dve.wait_ge(acc_hi, hi_count)
                hi, lo = (q_hi, q_lo) if kind == "q" else (k_hi, k_lo)
                cols = slice(c * HALF, (c + 1) * HALF)
                nc.vector.tensor_tensor(lo[:, par, cols], ACCB[c][:, :], hi[:, par, cols].bitcast(F32),
                                        ALU.subtract).then_inc(acc_free, 1)

            def v_copy(index, c):
                dve.wait_ge(acc_full, index + 1)
                nc.vector.tensor_copy(vT[:, c * HALF:(c + 1) * HALF], ACCB[c][:, :]).then_inc(acc_free, 1)

            for n, kind in enumerate("qk"):
                for c in range(2):
                    qk_lo(2 * n + c, 2 * n + c + 1, kind, 0, c)
            v_copy(4, 0)

            def out_add(index, t, c):
                dve.wait_ge(acc_full, index + 1)
                cols = slice(c * HALF, (c + 1) * HALF)
                nc.vector.tensor_tensor(acc[:, t, cols], ACCB[c][:, :], acc[:, t, cols],
                                        ALU.add).then_inc(acc_free, 1)

            O_SLOT = {2: (-1, 1, 0, 0), 3: (-1, 1, 0, 1), 6: (-1, 1, 1, 0), 7: (-1, 1, 1, 1),
                      18: (0, 0, 0, 0), 19: (0, 0, 0, 1), 25: (0, 0, 1, 0), 26: (0, 0, 1, 1)}

            def step(p, par, first=False, proj=True, wo=True, slots=SLOTS):
                tail = slots < SLOTS
                for s in range(slots):
                    if s in T_SLOT:
                        n, kind, h, j = T_SLOT[s]
                        g = t_index(p, n)
                        b = n % 2
                        if kind == "v" and not tail:
                            t_lo_sub(g, V[:, j:j + 4, :, 1, :],
                                     TB[b][:, :].rearrange("p (k h c) -> p k h c", k=4, h=2),
                                     V[:, j:j + 4, :, 0, :])
                        elif kind != "v" and not (kind == "prev" and first):
                            w = P * (min(j, 3) + 1 if kind == "lo" else j - 3)
                            t_lo_sub(g, AT_lo[:, b, 0:w], TB[b][:, 0:w], AT_hi[:, b, 0:w])
                    if s == 0 and not tail:
                        v_copy(acc_base(p) - 1 if not first else 5, 1)
                    if not tail and proj:
                        if s in (4, 8, 20, 24):
                            kind = "q" if s < 16 else "k"
                            c = 0 if s % 8 == 4 else 1
                            hi_count = 4 * p + 4 + (0 if kind == "q" else 2) + c + 1
                            qk_lo(step_units(p, kind)[0] + c, hi_count, kind, 1 - par, c)
                        if s == 28:
                            v_copy(step_units(p, "v")[0], 0)
                    if not tail and wo and 9 <= s <= 16:
                        if s == 9:
                            dve.wait_ge(acc_free, step_units(p, "wo")[0])
                        for c in range(2):
                            out_add(step_units(p, "wo")[0] + 2 * (s - 9) + c, s - 9, c)
                    if s in ROW_SLOT and not tail:
                        h, r = ROW_SLOT[s]
                        R = 16 * p + 8 * h + r
                        w = ROW_W[r]
                        st = stay[r % 2]
                        dve.wait_ge(mask_done, R + 1)
                        dve.wait_ge(sig_done, 2 * NCH * p + NCH * h + LAST_CHUNK[r] + 1)
                        nc.vector.tensor_tensor_scan(st[:, 1:1 + w], st[:, 1:1 + w], st[:, 1:1 + w], 1.0,
                                                     ALU.mult, ALU.bypass).then_inc(scan_done, 1)
                        dve.wait_ge(scan_done, R + 1)
                        a = A[r // 4][:, ROW_AT[r]:ROW_AT[r] + w]
                        nc.vector.tensor_tensor(a, a, st[:, 0:w], ALU.mult).then_inc(row_done, 1)
                    if s in O_SLOT and not (first and O_SLOT[s][0] < 0):
                        dp, h, half_q, half = O_SLOT[s]
                        rows = slice(HD * h, HD * (h + 1))
                        dve.wait_ge(o_half, 8 * (p + dp) + 4 * h + 2 * half_q + half + 1)
                        cols = slice(HALF * half_q + 256 * half, HALF * half_q + 256 * half + 256)
                        nc.vector.tensor_tensor(oT_hi[rows, cols], OB[half_q][0:HD, half * 256:half * 256 + 256],
                                                o_part[rows, :], ALU.add)
                        nc.vector.tensor_tensor(o_part[rows, :], OB[half_q][0:HD, half * 256:half * 256 + 256],
                                                o_part[rows, :], ALU.add).then_inc(o_sum, 1)
                        dve.wait_ge(o_sum, 8 * (p + dp) + 4 * h + 2 * half_q + half + 1)
                        nc.vector.tensor_tensor(oT_lo[rows, cols], o_part[rows, :], oT_hi[rows, cols].bitcast(F32),
                                                ALU.subtract).then_inc(o_lo, 1)

            step(0, 0, first=True, wo=False)
            with dve.Fori(0, PAIRS // 2 - 1) as i:
                for u in range(2):
                    step(2 * i + 1 + u, (1 + u) % 2)
            step(PAIRS - 1, 1, proj=False)
            step(PAIRS, 0, proj=False, wo=False, slots=8)

            dve.wait_ge(gain2_in, 32)
            dve.wait_ge(acc_free, ACC_END - 16)
            for k in range(NT + 4):
                if k < NT:
                    for c in range(2):
                        out_add(ACC_END - 16 + 2 * k + c, k, c)
                if 1 <= k <= NT:
                    t = k - 1
                    dve.wait_ge(rstd_done, NT + (2 * t if t else 0) + (1 if t == 0 else 0))
                    nc.vector.scalar_tensor_tensor(out=acc[:, t, :], in0=acc[:, t, :],
                                                   scalar=rstd[:, NT + t:NT + t + 1], in1=g_post_t[:, :],
                                                   op0=ALU.mult, op1=ALU.mult).then_inc(mix_scaled, 1)
                if 2 <= k <= NT + 1:
                    t = k - 2
                    dve.wait_ge(rstd_done, NT + 2 * t + 3 if t < NT - 1 else 3 * NT)
                    if t >= 2:
                        dve.wait_ge(t_full, T_TRANS + 2 * (t - 1))
                    nc.vector.scalar_tensor_tensor(out=hn_t[:, t % 2, :], in0=acc[:, t, :],
                                                   scalar=rstd[:, 2 * NT + t:2 * NT + t + 1],
                                                   in1=g_ffn_t[:, :], op0=ALU.mult,
                                                   op1=ALU.mult).then_inc(hn_ready, 1)
                if 3 <= k <= NT + 2:
                    t = k - 3
                    for half in range(2):
                        norm_lo(T_TRANS + 2 * t + half, t, half)

            def ffn_chunk(g, e, par, c):
                n = 4 * g + 2 * e + c
                dve.wait_ge(sg_ready, n + 1)
                nc.vector.tensor_tensor(sg[:, c, :], GATEB[c][:, :], sg[:, c, :], ALU.mult).then_inc(silu_ready, 1)
                dve.wait_ge(silu_ready, n + 1)
                nc.vector.tensor_tensor(sg[:, c, :], UPB[c][:, :], sg[:, c, :], ALU.mult).then_inc(prod_ready, 1)

            for e in range(2):
                for c in range(2):
                    ffn_chunk(0, e, 0, c)
            dve.wait_ge(y_zero, 1)

            def y_add(g, k):
                n = 16 * g + k
                dve.wait_ge(y_full, n + 1)
                cols = slice((k % 2) * HALF, (k % 2 + 1) * HALF)
                nc.vector.tensor_tensor(y[:, k // 2, cols], YB[k % 4][:, :], y[:, k // 2, cols],
                                        ALU.add).then_inc(y_free, 1)

            with dve.Fori(0, (NG - 1) // 2) as i:
                for u in range(2):
                    g, par = 2 * i + 1 + u, (1 + u) % 2
                    for c in range(2):
                        ffn_chunk(g, 0, par, c)
                    for c in range(2):
                        ffn_chunk(g, 1, par, c)
                    dve.wait_ge(prod_ready, 4 * g + 4)
                    for k in range(16):
                        y_add(g - 1, k)

            dve.wait_ge(y_free, 16 * (NG - 1))
            dve.wait_ge(gain3_in, 16)

            def finish(t):
                dve.wait_ge(rstd_done, 3 * NT + t + 1)
                nc.vector.scalar_tensor_tensor(out=y[:, t, :], in0=y[:, t, :], scalar=rstd[:, t:t + 1],
                                               in1=g_out[:, :], op0=ALU.mult, op1=ALU.mult).then_inc(y_scaled, 1)
                dve.wait_ge(y_scaled, t + 1)
                nc.vector.tensor_tensor(y[:, t, :], y[:, t, :], acc[:, t, :], ALU.add).then_inc(out_ready, 1)

            for t in range(NT + 1):
                if t < NT:
                    y_add(NG - 1, 2 * t)
                    y_add(NG - 1, 2 * t + 1)
                if t:
                    finish(t - 1)

        @block.tensor
        def _(pe):
            def project_tiles(c, slot, kts, index):
                for kt in kts:
                    wh = w_hi[slot][:, kt * P:(kt + 1) * P]
                    wl = w_lo[slot][:, kt * P:(kt + 1) * P]
                    cols = slice(c * HALF, (c + 1) * HALF)
                    nc.tensor.matmul(ACCB[c][:, :], wh, hnT_hi[:, kt, cols], start=(kt == 0), stop=False)
                    nc.tensor.matmul(ACCB[c][:, :], wh, hnT_lo[:, kt, cols], start=False, stop=False)
                    mm = nc.tensor.matmul(ACCB[c][:, :], wl, hnT_hi[:, kt, cols], start=False, stop=(kt == KT - 1))
                if kts[-1] == KT - 1:
                    mm.then_inc(acc_full, 1)

            def transpose_norm(n, src, half):
                if n >= 2:
                    pe.wait_ge(t_lo, n - 1)
                for q in range(4):
                    k = 4 * half + q
                    mm = nc.tensor.transpose(TB[n % 2][:, q * P:(q + 1) * P], src[:, k * P:(k + 1) * P], ident[:, :])
                mm.then_inc(t_full, 1)

            pe.wait_ge(consts, 7)
            for t in range(NT):
                pe.wait_ge(hn_ready, t + 1)
                for half in range(2):
                    transpose_norm(2 * t + half, hn_s[:, t % 2, :], half)

            for n in range(3):
                pe.wait_ge(w_ready, n + 1)
                for c in range(2):
                    if n == 0:
                        pe.wait_ge(t_lo, NT * (c + 1))
                    if n:
                        pe.wait_ge(acc_free, 2 * n + c - 1)
                    project_tiles(c, n % 2, range(KT), 2 * n + c)

            def out_project(index, t, slot):
                for c in range(2):
                    pe.wait_ge(acc_free, index + c - 1)
                    cols = slice(c * HALF, (c + 1) * HALF)
                    oh, ol = oT_hi[:, t * P:(t + 1) * P], oT_lo[:, t * P:(t + 1) * P]
                    nc.tensor.matmul(ACCB[c][:, :], oh, w_hi[slot][:, cols], start=True, stop=False)
                    nc.tensor.matmul(ACCB[c][:, :], oh, w_lo[slot][:, cols], start=False, stop=False)
                    nc.tensor.matmul(ACCB[c][:, :], ol, w_hi[slot][:, cols], start=False, stop=True
                                     ).then_inc(acc_full, 1)

            def step(p, par, first=False, proj=True, wo=True, slots=SLOTS):
                tail = slots < SLOTS
                for s in range(slots):
                    dp = 0
                    at = s - AV_LAG
                    if at < 0:
                        dp, at = -1, at + SLOTS
                    if at in T_SLOT and T_SLOT[at][1] != "v" and not (first and (dp < 0 or T_SLOT[at][1] == "prev")):
                        n, kind, h, j = T_SLOT[at]
                        half_q = 0 if kind == "lo" else 1
                        start = j == (0 if kind == "lo" else 4)
                        stop = j == NT - 1
                        w = P * (min(j, 3) + 1 if kind == "lo" else j - 3)
                        b = n % 2
                        if start:
                            sb = 4 * (p + dp) + 2 * h + half_q - (4 if kind == "prev" else 0)
                            if not (isinstance(sb, int) and sb < 2):
                                pe.wait_ge(o_sum, 2 * (sb - 1))
                        pe.wait_ge(t_lo, t_index(p + dp, n) + 1)
                        v = V[:, j, h, :, :].rearrange("p a c -> p (a c)")
                        nc.tensor.matmul(OB[half_q][:, 0:w], v, AT_hi[:, b, 0:w], start=start, stop=False,
                                         skip_group_check=True)
                        nc.tensor.matmul(OB[half_q][:, 0:w], v, AT_lo[:, b, 0:w], start=False, stop=stop,
                                         skip_group_check=True).then_inc(av_done, 1)
                    if s in T_SLOT:
                        n, kind, h, j = T_SLOT[s]
                        g = t_index(p, n)
                        b = n % 2
                        if kind == "v" and not tail:
                            pe.wait_ge(t_lo, g - 1)
                            if n == 4:
                                pe.wait_ge(acc_free, acc_base(p) if not first else 6)
                            for q in range(4):
                                mm = nc.tensor.transpose(TB[b][:, q * P:(q + 1) * P],
                                                         vT[:, (j + q) * P:(j + q + 1) * P], ident[:, :])
                            mm.then_inc(t_full, 1)
                        elif kind != "v" and not (kind == "prev" and first):
                            pe.wait_ge(t_lo, g - 1)
                            rows = range(0, min(j, 3) + 1) if kind == "lo" else range(4, j + 1)
                            hp = 16 * p + 8 * h - (16 if kind == "prev" else 0)
                            pe.wait_ge(row_done, hp + rows[-1] + 1)
                            for q, r in enumerate(rows):
                                at_ = ROW_AT[r] + (j - r) * P
                                mm = nc.tensor.transpose(TB[b][:, q * P:(q + 1) * P],
                                                         A[r // 4][:, at_:at_ + P], ident[:, :])
                            mm.then_inc(t_full, 1)
                    if s in Z_SLOT and not tail:
                        h, c = Z_SLOT[s]
                        r, a, e, _ = CHUNKS[c]
                        z = 2 * NCH * p + NCH * h + c
                        if s == 0:
                            pe.wait_ge(acc_free, 4 if first else acc_base(p) - 2)
                        if not (isinstance(z, int) and z < 2):
                            pe.wait_ge(sig_done, z - 1)
                        hr = slice(HD * h, HD * (h + 1))
                        qs, ks = slice(r * P, (r + 1) * P), slice(a, e)
                        dst = ZB[c % 2][:, 0:e - a]
                        nc.tensor.matmul(dst, q_hi[hr, par, qs], k_hi[hr, par, ks], start=True, stop=False)
                        nc.tensor.matmul(dst, q_hi[hr, par, qs], k_lo[hr, par, ks], start=False, stop=False)
                        nc.tensor.matmul(dst, q_lo[hr, par, qs], k_hi[hr, par, ks], start=False, stop=True
                                         ).then_inc(z_full, 1)
                    if not tail:
                        kind = FILL_KIND[s // 8]
                        if kind == "wo":
                            if wo:
                                index, n = step_units(p, "wo")
                                if s == 8:
                                    pe.wait_ge(w_ready, n + 1)
                                    pe.wait_ge(o_lo, 8 * p - 2)
                                if s == 12:
                                    pe.wait_ge(o_lo, 8 * p)
                                out_project(index + 2 * (s - 8), s - 8, unit_slot(p, "wo"))
                        elif proj:
                            index, n = step_units(p, kind)
                            c = (s % 8) // 4
                            if s % 8 == 0:
                                pe.wait_ge(w_ready, n + 1)
                            if s % 4 == 0:
                                pe.wait_ge(acc_free, index + c - 1)
                            k0 = 2 * (s % 4)
                            project_tiles(c, unit_slot(p, kind), range(k0, k0 + 2), index + c)

            step(0, 0, first=True, wo=False)
            with pe.Fori(0, PAIRS // 2 - 1) as i:
                for u in range(2):
                    step(2 * i + 1 + u, (1 + u) % 2)
            step(PAIRS - 1, 1, proj=False)
            step(PAIRS, 0, proj=False, wo=False, slots=8)

            pe.wait_ge(w_ready, UNITS1)
            for k in range(NT + 3):
                if k < NT:
                    if k == 0:
                        pe.wait_ge(o_lo, 8 * PAIRS - 2)
                    if k == 4:
                        pe.wait_ge(o_lo, 8 * PAIRS)
                    out_project(ACC_END - 16 + 2 * k, k, 1)
                if k >= 3:
                    t = k - 3
                    pe.wait_ge(hn_ready, NT + t + 1)
                    for half in range(2):
                        transpose_norm(T_TRANS + 2 * t + half, hn_t[:, t % 2, :], half)

            def gate_up(g, e, c, is_up, slot):
                dst = (UPB if is_up else GATEB)[c][:, :]
                cols = slice(c * HALF, (c + 1) * HALF)
                n = 4 * g + 2 * e + c
                if not is_up and not (isinstance(n, int) and n < 2):
                    pe.wait_ge(prod_ready, n - 1)
                for kt in range(KT):
                    wh = w_hi[slot][:, kt * P:(kt + 1) * P]
                    wl = w_lo[slot][:, kt * P:(kt + 1) * P]
                    nc.tensor.matmul(dst, wh, hnT_hi[:, kt, cols], start=(kt == 0), stop=False)
                    nc.tensor.matmul(dst, wh, hnT_lo[:, kt, cols], start=False, stop=False)
                    mm = nc.tensor.matmul(dst, wl, hnT_hi[:, kt, cols], start=False, stop=(kt == KT - 1))
                mm.then_inc(up_full if is_up else gate_full, 1)

            def down(g, par, slots, last=None):
                pe.wait_ge(h_ready, 4 * g + 4)
                for k in range(16):
                    t, c = k // 2, k % 2
                    cols = slice(c * HALF, (c + 1) * HALF)
                    n = 16 * g + k
                    if k >= 4 or last:
                        pe.wait_ge(y_free, n - 3)
                    for e in range(2):
                        hh = h_hi[:, par, e, t * P:(t + 1) * P]
                        hl = h_lo[:, par, e, t * P:(t + 1) * P]
                        wh, wl = w_hi[slots[e]][:, cols], w_lo[slots[e]][:, cols]
                        nc.tensor.matmul(YB[k % 4][:, :], hh, wh, start=(e == 0), stop=False)
                        nc.tensor.matmul(YB[k % 4][:, :], hh, wl, start=False, stop=False)
                        mm = nc.tensor.matmul(YB[k % 4][:, :], hl, wh, start=False, stop=(e == 1))
                    mm.then_inc(y_full, 1)

            for m in range(4):
                pe.wait_ge(w_ready, UNITS1 + m + 1)
                for c in range(2):
                    if m == 0:
                        pe.wait_ge(t_lo, T_TRANS + NT * (c + 1))
                    gate_up(0, m // 2, c, m % 2 == 1, m % 3)

            with pe.Fori(0, (NG - 1) // 2) as i:
                for u in range(2):
                    g, par, m_mod = 2 * i + 1 + u, (1 + u) % 2, (4 + 6 * u) % 3
                    base = UNITS1 + 6 * g - 2
                    for m in range(4):
                        pe.wait_ge(w_ready, base + m + 1)
                        for c in range(2):
                            gate_up(g, m // 2, c, m % 2 == 1, (m_mod + m) % 3)
                    pe.wait_ge(w_ready, base + 6)
                    down(g - 1, 1 - par, [(m_mod + 4) % 3, (m_mod + 5) % 3])
            pe.wait_ge(w_ready, UNITS)
            m = 6 * (NG - 1) + 4
            down(NG - 1, (NG - 1) % 2, [m % 3, (m + 1) % 3], last=True)


def kernel(**inputs):
    import numpy as _np
    import concourse.bacc as _bacc
    from concourse import mybir as _mybir
    from concourse.bass_utils import run_bass_kernel_spmd as _run

    a = {k: _np.asarray(v) for k, v in inputs.items()}

    def col_units(w, n):
        return w[:, n * P:(n + 1) * P].reshape(KT, P, P).transpose(1, 0, 2).reshape(P, D)

    w_qkv, w_o, w_gu, w_down = a["sb_w_qkv"][0], a["sb_w_o"][0], a["ffn_w_gu"][0], a["ffn_w_down"][0]
    q = [col_units(w_qkv, p) for p in range(PAIRS)]
    k = [col_units(w_qkv, PAIRS + p) for p in range(PAIRS)]
    v = [col_units(w_qkv, 2 * PAIRS + p) for p in range(PAIRS)]
    wo = [w_o[p * P:(p + 1) * P] for p in range(PAIRS)]
    gate = [col_units(w_gu, f) for f in range(NF)]
    up = [col_units(w_gu, NF + f) for f in range(NF)]
    down = [w_down[f * P:(f + 1) * P] for f in range(NF)]
    order = [q[0], k[0], v[0], q[1], k[1], v[1]]
    for p in range(1, PAIRS - 1):
        order += [q[p + 1], wo[p - 1], k[p + 1], v[p + 1]]
    order += [wo[PAIRS - 2], wo[PAIRS - 1], gate[0], up[0], gate[1], up[1]]
    for g in range(1, NG):
        order += [gate[2 * g], up[2 * g], gate[2 * g + 1], up[2 * g + 1], down[2 * g - 2], down[2 * g - 1]]
    order += [down[NF - 2], down[NF - 1]]

    arrays = {
        "in_x": _np.ascontiguousarray(a["x"][:, ::-1]),
        "in_mix_pre": _np.ascontiguousarray(a["ln_mix_pre"][0]),
        "in_mix_post": _np.ascontiguousarray(a["ln_mix_post"][0]),
        "in_ffn_pre": _np.ascontiguousarray(a["ln_ffn_pre"][0]),
        "in_ffn_post": _np.ascontiguousarray(a["ln_ffn_post"][0]),
        "in_units": _np.ascontiguousarray(_np.stack(order)),
    }
    nc = _bacc.Bacc("TRN2", target_bir_lowering=False, num_devices=1)
    args = [nc.dram_tensor(n, t.shape, _mybir.dt.from_np(t.dtype), kind="ExternalInput").ap()
            for n, t in arrays.items()]
    args.append(nc.dram_tensor("out_0", a["x"].shape, _mybir.dt.float32, kind="ExternalOutput").ap())
    encoder_layer(nc, *args)
    r = _run(nc, [arrays], core_ids=[0])
    return _np.ascontiguousarray(_np.asarray(r.results[0]["out_0"])[:, ::-1])
```

```python
from contextlib import ExitStack

import concourse.bass as bass
from concourse import mybir

F32 = mybir.dt.float32
F32R = mybir.dt.float32r
ALU = mybir.AluOpType
ACT = mybir.ActivationFunctionType

P = 128
D = 1024
SEQ = 1024
KT = D // P
NT = SEQ // P
HALF = 512
HD = 64
PAIRS = D // (2 * HD)
D_FF = ((8 * D + 3 * 256 - 1) // (3 * 256)) * 256
NF = D_FF // P
NG = NF // 2
Z_SCALE = HD ** -0.5
EPS = 1e-6
UNITS1 = 4 * PAIRS
UNITS = UNITS1 + 3 * NF
SLOTS = 32

ROW_W = [SEQ - P * r for r in range(NT)]
ROW_AT = [sum(ROW_W[:r]) if r < 4 else sum(ROW_W[4:r]) for r in range(NT)]
A_SIZE = [sum(ROW_W[:4]), sum(ROW_W[4:])]


def row_chunks(r):
    return [(P * r, HALF), (HALF, SEQ)] if r < 4 else [(P * r, SEQ)]


CHUNKS = [(r, a, b, n == len(row_chunks(r)) - 1) for r in range(NT) for n, (a, b) in enumerate(row_chunks(r))]
NCH = len(CHUNKS)
LAST_CHUNK = [max(n for n, c in enumerate(CHUNKS) if c[0] == r) for r in range(NT)]

Z_SLOT = {16 * h + c: (h, c) for h in range(2) for c in range(NCH)}
ROW_SLOT = {16 * h + LAST_CHUNK[r] + 1: (h, r) for h in range(2) for r in range(NT)}
T_SLOT = {}
for _n, _s in enumerate((0, 1, 2, 3)):
    T_SLOT[_s] = (_n, "prev", 1, 4 + _n)
for _n, _s in enumerate((6, 7)):
    T_SLOT[_s] = (4 + _n, "v", 0, 4 * _n)
for _n in range(8):
    T_SLOT[8 + _n] = (6 + _n, "lo", 0, _n)
    T_SLOT[24 + _n] = (18 + _n, "lo", 1, _n)
for _n, _s in enumerate((16, 18, 20, 22)):
    T_SLOT[_s] = (14 + _n, "up", 0, 4 + _n)
T_PER_STEP = 26
T_START = 2 * NT
AV_LAG = 2


def t_index(p, n):
    return T_START - 4 + T_PER_STEP * p + n


def av_index(p, kind, h, j):
    if kind == "prev":
        return 2 * NCH * p - 4 + (j - 4)
    return 2 * NCH * p + NCH * h + (j if kind == "lo" else 8 + j - 4)


def t_of_av(p, kind, h, j):
    n = next(v[0] for v in T_SLOT.values() if v[1:] == (kind, h, j))
    return t_index(p, n)


def acc_base(p):
    return 6 if isinstance(p, int) and p == 0 else 12 + 22 * (p - 1)


def unit_base(p):
    return 3 if isinstance(p, int) and p == 0 else 6 + 4 * (p - 1)


ACC_OFF = {"q": 0, "wo": 2, "k": 18, "v": 20}
UNIT_OFF = {"q": 0, "wo": 1, "k": 2, "v": 3}


def step_units(p, kind):
    if isinstance(p, int) and p == 0:
        n = {"q": 0, "k": 1, "v": 2}[kind]
        return 6 + 2 * n, 3 + n
    if isinstance(p, int) and p >= PAIRS - 1:
        return acc_base(PAIRS - 1) + 16 * (p - (PAIRS - 1)), unit_base(PAIRS - 1) + p - (PAIRS - 1)
    return acc_base(p) + ACC_OFF[kind], unit_base(p) + UNIT_OFF[kind]


def unit_slot(p, kind):
    if isinstance(p, int):
        return step_units(p, kind)[1] % 2
    return UNIT_OFF[kind] % 2


ACC_END = 12 + 22 * (PAIRS - 2) + 32
T_TRANS = T_START - 4 + T_PER_STEP * PAIRS + 4
T_END = T_TRANS + 2 * NT
FILL_KIND = ["q", "wo", "k", "v"]
O_SLOT = {2: (-1, 1, 0, 0), 3: (-1, 1, 0, 1), 6: (-1, 1, 1, 0), 7: (-1, 1, 1, 1),
          18: (0, 0, 0, 0), 19: (0, 0, 0, 1), 25: (0, 0, 1, 0), 26: (0, 0, 1, 1)}
FIRST_ACC = [("q", 0), ("k", 0), ("q", 1), ("k", 1), ("v", 0), ("v", 1)]
NORM_LAG = 3


def encoder_layer(nc, x, g_mix_pre, g_mix_post, g_ffn_pre, g_ffn_post, units, out):
    ctx = ExitStack()
    with ctx:
        def sem(name):
            return ctx.enter_context(nc.semaphore(name))

        def alloc(stack, name, shape, dt=F32):
            return stack.enter_context(nc.sbuf_tensor(name, shape, dt))

        hnT_hi = alloc(ctx, "hnT_hi", [P, KT, SEQ], F32R)
        hnT_lo = alloc(ctx, "hnT_lo", [P, KT, SEQ], F32R)
        acc = alloc(ctx, "acc", [P, NT, D])
        raw = alloc(ctx, "raw", [P, 2, D])
        w_hi01 = alloc(ctx, "w_hi01", [P, 2, D], F32R)
        w_lo01 = alloc(ctx, "w_lo01", [P, 2, D], F32R)
        ident = alloc(ctx, "ident", [P, P])
        keep = alloc(ctx, "keep", [P, P], mybir.dt.bfloat16)
        ss = alloc(ctx, "ss", [P, 4 * NT])
        ms = alloc(ctx, "ms", [P, 3 * NT])
        rstd = alloc(ctx, "rstd", [P, 3 * NT])
        mhalf = alloc(ctx, "mhalf", [P, 1])

        with ExitStack() as one:
            A = [alloc(one, f"A{n}", [P, A_SIZE[n]]) for n in range(2)]
            with ExitStack() as qk:
                q_hi = alloc(qk, "q_hi", [P, 2, SEQ], F32R)
                q_lo = alloc(qk, "q_lo", [P, 2, SEQ], F32R)
                k_hi = alloc(qk, "k_hi", [P, 2, SEQ], F32R)
                k_lo = alloc(qk, "k_lo", [P, 2, SEQ], F32R)
                V = alloc(qk, "V", [P, NT, 2, 2, HD], F32R)
                vT = alloc(qk, "vT", [P, SEQ])
                stay = [alloc(qk, "stay0", [P, 1 + SEQ]), alloc(qk, "stay1", [P, 1 + SEQ - P])]
                AT_hi = alloc(qk, "AT_hi", [P, 2, HALF], F32R)
                AT_lo = alloc(qk, "AT_lo", [P, 2, HALF], F32R)
                oT_hi = alloc(qk, "oT_hi", [P, SEQ], F32R)
                oT_lo = alloc(qk, "oT_lo", [P, SEQ], F32R)
                o_part = alloc(qk, "o_part", [P, HALF // 2])
            with ExitStack() as tr:
                g_post_t = alloc(tr, "g_post_t", [P, D])
                g_ffn_t = alloc(tr, "g_ffn_t", [P, D])
                x_in = alloc(tr, "x_in", [P, 2, D])
                hn_t = alloc(tr, "hn_t", [P, 2, D])
                junk_t = alloc(tr, "junk_t", [P, D])
        with ExitStack() as st:
            g_pre_s = alloc(st, "g_pre_s", [P, D])
            hn_s = alloc(st, "hn_s", [P, 2, D])
            junk_s = alloc(st, "junk_s", [P, D])
        with ExitStack() as two:
            w_hi2 = alloc(two, "w_hi2", [P, D], F32R)
            w_lo2 = alloc(two, "w_lo2", [P, D], F32R)
            g_out = alloc(two, "g_out", [P, D])
            sg = alloc(two, "sg", [P, 2, HALF])
            alloc(two, "gap", [P, sum(A_SIZE) - 4 * D])
            y = alloc(two, "y", [P, NT, D])
            h_hi = alloc(two, "h_hi", [P, 2, 2, SEQ], F32R)
            h_lo = alloc(two, "h_lo", [P, 2, 2, SEQ], F32R)

        bank = [ctx.enter_context(nc.psum_tensor(f"bank{n}", [P, HALF], F32)) for n in range(8)]
        ACCB = bank[0:2]
        ZB = bank[2:4]
        TB = bank[4:6]
        OB = bank[6:8]
        GATEB, UPB = ZB, OB
        YB = ACCB + TB
        FIRST_GATE_B = [ZB[0], ACCB[0], ZB[1], ACCB[1]]

        w_hi = [w_hi01[:, 0, :], w_hi01[:, 1, :], w_hi2[:, :]]
        w_lo = [w_lo01[:, 0, :], w_lo01[:, 1, :], w_lo2[:, :]]

        x_tile = [sem(f"x_tile{t}") for t in range(NT)]
        raw_in = [sem("raw_in0"), sem("raw_in1")]
        gain_in = sem("gain_in")
        gain2_in = sem("gain2_in")
        gain3_in = sem("gain3_in")
        x_again = [sem("x_again0"), sem("x_again1")]
        out_done = sem("out_done")
        consts = sem("consts")
        w_hi_ready = sem("w_hi_ready")
        w_ready = sem("w_ready")
        sq_done = sem("sq_done")
        ms_done = sem("ms_done")
        rstd_done = sem("rstd_done")
        hn_ready = sem("hn_ready")
        mix_scaled = sem("mix_scaled")
        x2_ready = sem("x2_ready")
        t_full = sem("t_full")
        t_hi = sem("t_hi")
        t_lo = sem("t_lo")
        acc_full = sem("acc_full")
        acc_hi = sem("acc_hi")
        acc_free = sem("acc_free")
        z_full = sem("z_full")
        sig_done = sem("sig_done")
        mask_done = sem("mask_done")
        scan_done = sem("scan_done")
        row_done = sem("row_done")
        av_done = sem("av_done")
        o_half = sem("o_half")
        o_sum = sem("o_sum")
        o_lo = sem("o_lo")
        gate_full = sem("gate_full")
        up_full = sem("up_full")
        sg_ready = sem("sg_ready")
        silu_ready = sem("silu_ready")
        prod_ready = sem("prod_ready")
        h_hi_ready = sem("h_hi_ready")
        h_ready = sem("h_ready")
        y_zero = sem("y_zero")
        y_full = sem("y_full")
        y_free = sem("y_free")
        ysq_done = sem("ysq_done")
        y_scaled = sem("y_scaled")
        out_ready = sem("out_ready")

        x_tiles = x.rearrange("b (t p) d -> p (b t) d", p=P)
        out_tiles = out.rearrange("b (t p) d -> p (b t) d", p=P)

        block = ctx.enter_context(nc.Block())

        def before_count(p, kind):
            return step_units(p, kind)[0]

        @block.sync
        def _(sp):
            for t in range(4):
                sp.dma_start(acc[:, t, :], x_tiles[:, t, :]).then_inc(x_tile[t], 16)
            sp.dma_start(raw[:, 0, :], units[0]).then_inc(raw_in[0], 16)
            for t in range(4, NT):
                sp.dma_start(acc[:, t, :], x_tiles[:, t, :]).then_inc(x_tile[t], 16)
            sp.dma_start(raw[:, 1, :], units[1]).then_inc(raw_in[1], 16)
            with sp.Fori(1, UNITS // 2) as i:
                for s in range(2):
                    sp.wait_ge(w_ready, 2 * i + s - 1)
                    sp.dma_start(raw[:, s, :], units[bass.ds(2 * i + s, 1)].rearrange("a p n -> p (a n)")
                                 ).then_inc(raw_in[s], 16)
            for t in range(NT):
                sp.wait_ge(out_ready, t + 1)
                sp.dma_start(out_tiles[:, t, :], y[:, t, :]).then_inc(out_done, 16)
            sp.wait_ge(out_done, 16 * NT)

        @block.scalar
        def _(act):
            def split_hi(n, slot, raw_slot, count):
                act.wait_ge(raw_in[raw_slot], count)
                nc.scalar.activation(w_hi[slot], raw[:, raw_slot, :], ACT.Copy).then_inc(w_hi_ready, 1)

            def raw_count(n, parity):
                return 16 * (n // 2 + 1) if isinstance(n, int) else 8 * (n - parity) + 16

            def t_hi_copy(index, par, out_ap, in_ap):
                act.wait_ge(t_full, index + 1)
                nc.scalar.activation(out_ap, in_ap, ACT.Copy).then_inc(t_hi, 1)

            act.dma_start(g_pre_s[:, :], g_mix_pre.partition_broadcast(P)).then_inc(gain_in, 16)

            def start_hi(t):
                for half in range(2):
                    n = 2 * t + half
                    t_hi_copy(n, n % 2, hnT_hi[:, 4 * half:4 * half + 4, t * P:(t + 1) * P],
                              TB[n % 2][:, :].rearrange("p (k c) -> p k c", k=4))

            for t in range(NT):
                act.wait_ge(x_tile[t], 16)
                if t:
                    act.wait_ge(sq_done, t)
                nc.scalar.activation(junk_s[:, :], acc[:, t, :], ACT.Square,
                                     accum_out=ss[:, t:t + 1]).then_inc(sq_done, 1)
                if t == 3:
                    split_hi(0, 0, 0, 16)
                if t == 6:
                    split_hi(1, 1, 1, 16)
                if t >= 2:
                    start_hi(t - 2)
            start_hi(NT - 2)
            start_hi(NT - 1)

            def qk_hi(index, kind, par, c, b):
                act.wait_ge(acc_full, index + 1)
                dst = q_hi if kind == "q" else k_hi
                nc.scalar.activation(dst[:, par, c * HALF:(c + 1) * HALF], ACCB[b][:, :],
                                     ACT.Copy).then_inc(acc_hi, 1)

            for n, (kind, c) in enumerate(FIRST_ACC[:4]):
                qk_hi(n, kind, 0, c, n % 2)
                if n >= 2:
                    split_hi(n, n % 2, n % 2, raw_count(n, 0))

            def split_slot(p, s):
                st = s // 8
                kind = FILL_KIND[st]
                if isinstance(p, int) and p == 0:
                    if kind == "wo":
                        return
                    n = {"q": 4, "k": 5, "v": 6}[kind]
                    act.wait_ge(acc_full, before_count(p, kind))
                    split_hi(n, n % 2, n % 2, raw_count(n, 0))
                elif isinstance(p, int) and p == PAIRS - 1:
                    if kind == "wo":
                        act.wait_ge(acc_full, before_count(p, kind))
                        split_hi(31, 1, 1, raw_count(31, 1))
                else:
                    n = unit_base(p) + UNIT_OFF[kind] + 1
                    par = (UNIT_OFF[kind] + 1) % 2
                    act.wait_ge(acc_full, before_count(p, kind))
                    split_hi(n, par, par, raw_count(n, par))

            def o_copy(p, h, half_q, half):
                sb = 4 * p + 2 * h + half_q
                act.wait_ge(av_done, 2 * NCH * p + NCH * h + (NCH if half_q else 8))
                if not (isinstance(sb, int) and sb == 0 and half == 0):
                    act.wait_ge(o_lo, 2 * sb + half)
                rows = slice(HD * h, HD * (h + 1))
                nc.scalar.activation(o_part[rows, :], OB[half_q][HD:P, half * 256:half * 256 + 256],
                                     ACT.Copy).then_inc(o_half, 1)

            def step(p, par, first=False, proj=True, wo=True, slots=SLOTS):
                for s in range(slots):
                    tail = slots < SLOTS
                    if s in T_SLOT:
                        n, kind, h, j = T_SLOT[s]
                        g = t_index(p, n)
                        b = n % 2
                        if kind == "v" and not tail:
                            if not first:
                                act.wait_ge(av_done, 2 * NCH * p)
                            t_hi_copy(g, b, V[:, j:j + 4, :, 0, :],
                                      TB[b][:, :].rearrange("p (k h c) -> p k h c", k=4, h=2))
                        elif kind != "v" and not (kind == "prev" and first):
                            a = av_index(p, kind, h, j)
                            if not (isinstance(a, int) and a < 2):
                                act.wait_ge(av_done, a - 1)
                            w = P * (min(j, 3) + 1 if kind == "lo" else j - 3)
                            t_hi_copy(g, b, AT_hi[:, b, 0:w], TB[b][:, 0:w])
                    if s in Z_SLOT and not tail:
                        h, c = Z_SLOT[s]
                        r, a, e, _ = CHUNKS[c]
                        z = 2 * NCH * p + NCH * h + c
                        R = 16 * p + 8 * h + r
                        if (c == 0 or CHUNKS[c - 1][0] != r) and not (isinstance(R, int) and R < 2):
                            act.wait_ge(row_done, R - 1)
                        act.wait_ge(z_full, z + 1)
                        at = ROW_AT[r] + a - P * r
                        nc.scalar.activation(A[r // 4][:, at:at + e - a], ZB[c % 2][:, 0:e - a],
                                             ACT.Sigmoid, scale=Z_SCALE)
                        nc.scalar.activation(stay[r % 2][:, 1 + a - P * r:1 + e - P * r], ZB[c % 2][:, 0:e - a],
                                             ACT.Sigmoid, scale=-Z_SCALE).then_inc(sig_done, 1)
                    if proj and s in (4, 8, 20, 24) and not tail:
                        kind = "q" if s < 16 else "k"
                        c = 0 if s % 8 == 4 else 1
                        qk_hi(step_units(p, kind)[0] + c, kind, 1 - par, c, c)
                    if s in O_SLOT and not (first and O_SLOT[s][0] < 0):
                        dp, h, half_q, half = O_SLOT[s]
                        o_copy(p + dp, h, half_q, half)
                    if s % 8 == 1 and not tail:
                        split_slot(p, s)
                    if tail and s >= 4:
                        norm(s - 4)

            step(0, 0, first=True, wo=False)
            with act.Fori(0, PAIRS // 2 - 1) as i:
                for u in range(2):
                    step(2 * i + 1 + u, (1 + u) % 2)
            step(PAIRS - 1, 1, proj=False)

            def split_at(m, waits):
                for s, v in waits:
                    act.wait_ge(s, v)
                split_hi(UNITS1 + m, m % 3, m % 2, 16 * ((UNITS1 + m) // 2 + 1))

            def norm(k):
                if k < NT:
                    act.wait_ge(acc_free, ACC_END - 16 + 2 * (k + 1))
                    act.wait_ge(sq_done, NT + (2 * k - 1 if k else 0))
                    nc.scalar.activation(junk_t[:, :], acc[:, k, :], ACT.Square,
                                         accum_out=ss[:, NT + k:NT + k + 1]).then_inc(sq_done, 1)
                if 1 <= k <= NT:
                    act.wait_ge(x2_ready, k)
                    if k + 1 < NT:
                        act.dma_start(x_in[:, (k + 1) % 2, :], x_tiles[:, k + 1, :]
                                      ).then_inc(x_again[(k + 1) % 2], 16)
                    act.wait_ge(sq_done, NT + 2 * k if k < NT else 3 * NT - 1)
                    nc.scalar.activation(junk_t[:, :], acc[:, k - 1, :], ACT.Square,
                                         accum_out=ss[:, 2 * NT + k - 1:2 * NT + k]).then_inc(sq_done, 1)
                if k >= NORM_LAG:
                    t = k - NORM_LAG
                    for half in range(2):
                        n = T_TRANS + 2 * t + half
                        t_hi_copy(n, n % 2, hnT_hi[:, 4 * half:4 * half + 4, t * P:(t + 1) * P],
                                  TB[n % 2][:, :].rearrange("p (k c) -> p k c", k=4))

            act.wait_ge(z_full, 2 * NCH * PAIRS)
            act.dma_start(g_post_t[:, :], g_mix_post.partition_broadcast(P)).then_inc(gain2_in, 16)
            act.dma_start(g_ffn_t[:, :], g_ffn_pre.partition_broadcast(P)).then_inc(gain2_in, 16)
            for t in range(2):
                act.dma_start(x_in[:, t, :], x_tiles[:, t, :]).then_inc(x_again[t], 16)
            step(PAIRS, 0, proj=False, slots=8)
            for k in range(4, NT + NORM_LAG):
                if k == 4:
                    split_at(0, [(acc_full, ACC_END - 16)])
                if k == NT:
                    split_at(1, [(acc_full, ACC_END)])
                if k == NT + 1:
                    split_at(2, [])
                norm(k)
            act.dma_start(g_out[:, :], g_ffn_post.partition_broadcast(P)).then_inc(gain3_in, 16)

            def ffn_chunk(g, e, par, c):
                n = 4 * g + 2 * e + c
                act.wait_ge(up_full, n + 1)
                if not (isinstance(n, int) and n < 2):
                    act.wait_ge(h_ready, n - 1)
                gate_b = FIRST_GATE_B[2 * e + c] if isinstance(g, int) and g == 0 else GATEB[c]
                nc.scalar.activation(sg[:, c, :], gate_b[:, :], ACT.Sigmoid).then_inc(sg_ready, 1)
                act.wait_ge(prod_ready, n + 1)
                nc.scalar.activation(h_hi[:, par, e, c * HALF:(c + 1) * HALF], sg[:, c, :],
                                     ACT.Copy).then_inc(h_hi_ready, 1)

            ffn_chunk(0, 0, 0, 0)
            split_at(3, [(gate_full, 3)])
            ffn_chunk(0, 0, 0, 1)
            split_at(4, [(up_full, 2)])
            for c in range(2):
                ffn_chunk(0, 1, 0, c)

            def ffn_step(g, par, m_mod):
                base = 6 * g - 2

                def split(off, s, count):
                    act.wait_ge(s, count)
                    n = UNITS1 + base + off
                    rp = off % 2
                    rc = 16 * (n // 2 + 1) if isinstance(n, int) else 8 * (n - rp) + 16
                    split_hi(n, (m_mod + off) % 3, rp, rc)

                split(1, gate_full, 4 * g + 1)
                split(2, gate_full, 4 * g + 1)
                split(3, gate_full, 4 * g + 2)
                ffn_chunk(g, 0, par, 0)
                split(4, up_full, 4 * g + 2)
                ffn_chunk(g, 0, par, 1)
                split(5, gate_full, 4 * g + 4)
                ffn_chunk(g, 1, par, 0)
                split(6, up_full, 4 * g + 4)
                ffn_chunk(g, 1, par, 1)

            with act.Fori(0, (NG - 1) // 2) as i:
                for u in range(2):
                    ffn_step(2 * i + 1 + u, (1 + u) % 2, (4 + 6 * u) % 3)
            act.wait_ge(y_full, 16 * (NG - 1))
            m = 6 * (NG - 1) + 5
            split_hi(UNITS1 + m, m % 3, m % 2, 16 * ((UNITS1 + m) // 2 + 1))
            for t in range(NT):
                act.wait_ge(y_free, 16 * (NG - 1) + 2 * t + 2)
                for c in range(2):
                    if t or c:
                        act.wait_ge(ysq_done, 2 * t + c)
                    nc.scalar.activation(sg[:, c, :], y[:, t, c * HALF:(c + 1) * HALF], ACT.Square,
                                         accum_out=ss[:, (2 * t + c):(2 * t + c) + 1]).then_inc(ysq_done, 1)

        @block.gpsimd
        def _(pool):
            nc.gpsimd.memset(ident[:, :], 0.0).then_inc(consts, 1)
            nc.gpsimd.memset(mhalf[:, :], -0.5).then_inc(consts, 1)
            for b in range(2):
                nc.gpsimd.memset(stay[b][:, 0:1], 1.0).then_inc(consts, 1)
            nc.gpsimd.memset(keep[:, :], 1.0).then_inc(consts, 1)
            pool.wait_ge(consts, 5)
            nc.gpsimd.affine_select(out=ident[:, :], in_=ident[:, :], compare_op=ALU.not_equal, fill=1.0,
                                    base=0, pattern=[[-1, P]], channel_multiplier=1).then_inc(consts, 1)
            nc.gpsimd.affine_select(out=keep[:, :], in_=keep[:, :], compare_op=ALU.is_gt, fill=0.0,
                                    base=0, pattern=[[1, P]], channel_multiplier=-1).then_inc(consts, 1)
            pool.wait_ge(consts, 7)

            def split_lo(n, slot, raw_slot):
                pool.wait_ge(w_hi_ready, n + 1)
                nc.gpsimd.tensor_tensor(w_lo[slot], raw[:, raw_slot, :], w_hi[slot].bitcast(F32),
                                        ALU.subtract).then_inc(w_ready, 1)

            def inverse_rms(col, count):
                nc.gpsimd.tensor_scalar(ms[:, col:col + 1], ss[:, col:col + 1], 1.0 / D, EPS,
                                        ALU.mult, ALU.add).then_inc(ms_done, 1)
                pool.wait_ge(ms_done, count + 1)
                nc.gpsimd.tensor_tensor(rstd[:, col:col + 1], ms[:, col:col + 1], mhalf[:, :],
                                        ALU.pow).then_inc(rstd_done, 1)

            for t in range(NT):
                pool.wait_ge(sq_done, t + 1)
                inverse_rms(t, t)
                if t == 4:
                    split_lo(0, 0, 0)
            split_lo(1, 1, 1)
            split_lo(2, 0, 0)
            split_lo(3, 1, 1)

            def step(p, par, first=False, proj=True, slots=SLOTS):
                tail = slots < SLOTS
                for s in range(slots):
                    if s in Z_SLOT and not tail:
                        h, c = Z_SLOT[s]
                        r, a, _, _ = CHUNKS[c]
                        if a == P * r:
                            pool.wait_ge(sig_done, 2 * NCH * p + NCH * h + c + 1)
                            diag = A[r // 4][:, ROW_AT[r]:ROW_AT[r] + P]
                            nc.gpsimd.tensor_tensor(diag, diag, keep[:, :], ALU.mult)
                            diag = stay[r % 2][:, 1:1 + P]
                            nc.gpsimd.affine_select(out=diag, in_=diag, compare_op=ALU.is_gt, fill=1.0, base=0,
                                                    pattern=[[1, P]], channel_multiplier=-1).then_inc(mask_done, 1)
                    if s % 8 == 1 and not tail:
                        kind = FILL_KIND[s // 8]
                        if isinstance(p, int) and p == 0:
                            if kind != "wo":
                                n = {"q": 4, "k": 5, "v": 6}[kind]
                                split_lo(n, n % 2, n % 2)
                        elif isinstance(p, int) and p == PAIRS - 1:
                            if kind == "wo":
                                split_lo(31, 1, 1)
                        else:
                            q = (UNIT_OFF[kind] + 1) % 2
                            split_lo(unit_base(p) + UNIT_OFF[kind] + 1, q, q)

            step(0, 0, first=True)
            with pool.Fori(0, PAIRS // 2 - 1) as i:
                for u in range(2):
                    step(2 * i + 1 + u, (1 + u) % 2)
            step(PAIRS - 1, 1, proj=False)
            for k in range(NT + 1):
                if k < NT:
                    pool.wait_ge(sq_done, NT + (2 * k if k else 1))
                    inverse_rms(NT + k, NT + (2 * k - 1 if k else 0))
                if k == 4:
                    split_lo(UNITS1, 0, 0)
                if k == NT:
                    split_lo(UNITS1 + 1, 1, 1)
                if 1 <= k <= NT:
                    t = k - 1
                    pool.wait_ge(mix_scaled, t + 1)
                    pool.wait_ge(x_again[t % 2], 16 * (t // 2 + 1))
                    nc.gpsimd.tensor_tensor(acc[:, t, :], acc[:, t, :], x_in[:, t % 2, :],
                                            ALU.add).then_inc(x2_ready, 1)
                    pool.wait_ge(sq_done, NT + 2 * k + 1 if k < NT else 3 * NT)
                    inverse_rms(2 * NT + t, NT + 2 * k if k < NT else 3 * NT - 1)
            split_lo(UNITS1 + 2, 2, 0)
            pool.wait_ge(hn_ready, 2 * NT)
            pool.wait_ge(t_lo, T_END)
            nc.gpsimd.memset(y[:, :, :], 0.0).then_inc(y_zero, 1)

            def h_lo_chunk(g, e, par, c):
                n = 4 * g + 2 * e + c
                pool.wait_ge(h_hi_ready, n + 1)
                cols = slice(c * HALF, (c + 1) * HALF)
                nc.gpsimd.tensor_tensor(h_lo[:, par, e, cols], sg[:, c, :], h_hi[:, par, e, cols].bitcast(F32),
                                        ALU.subtract).then_inc(h_ready, 1)

            h_lo_chunk(0, 0, 0, 0)
            split_lo(UNITS1 + 3, 0, 1)
            h_lo_chunk(0, 0, 0, 1)
            split_lo(UNITS1 + 4, 1, 0)
            for c in range(2):
                h_lo_chunk(0, 1, 0, c)
            with pool.Fori(0, (NG - 1) // 2) as i:
                for u in range(2):
                    g, par, m_mod = 2 * i + 1 + u, (1 + u) % 2, (4 + 6 * u) % 3
                    base = UNITS1 + 6 * g - 2
                    for off in (1, 2, 3):
                        split_lo(base + off, (m_mod + off) % 3, off % 2)
                    for off in (4, 5, 6, None):
                        e, c = (0, 0) if off == 4 else (0, 1) if off == 5 else (1, 0) if off == 6 else (1, 1)
                        h_lo_chunk(g, e, par, c)
                        if off:
                            split_lo(base + off, (m_mod + off) % 3, off % 2)
            m = 6 * (NG - 1) + 5
            split_lo(UNITS1 + m, m % 3, m % 2)
            for t in range(NT):
                pool.wait_ge(ysq_done, 2 * t + 2)
                nc.gpsimd.tensor_tensor(ss[:, 3 * NT + t:3 * NT + t + 1], ss[:, 2 * t:2 * t + 1],
                                        ss[:, 2 * t + 1:2 * t + 2], ALU.add).then_inc(ms_done, 1)
                pool.wait_ge(ms_done, 3 * NT + 2 * t + 1)
                nc.gpsimd.tensor_scalar(ms[:, t:t + 1], ss[:, 3 * NT + t:3 * NT + t + 1], 1.0 / D, EPS,
                                        ALU.mult, ALU.add).then_inc(ms_done, 1)
                pool.wait_ge(ms_done, 3 * NT + 2 * t + 2)
                nc.gpsimd.tensor_tensor(rstd[:, t:t + 1], ms[:, t:t + 1], mhalf[:, :],
                                        ALU.pow).then_inc(rstd_done, 1)

        @block.vector
        def _(dve):
            def t_lo_sub(index, out_ap, in_ap, hi_ap):
                dve.wait_ge(t_hi, index + 1)
                nc.vector.tensor_tensor(out_ap, in_ap, hi_ap.bitcast(F32), ALU.subtract).then_inc(t_lo, 1)

            def norm_lo(index, t, half):
                ks, cols = slice(4 * half, 4 * half + 4), slice(t * P, (t + 1) * P)
                t_lo_sub(index, hnT_lo[:, ks, cols], TB[index % 2][:, :].rearrange("p (k c) -> p k c", k=4),
                         hnT_hi[:, ks, cols])

            dve.wait_ge(gain_in, 16)
            for t in range(NT + 1):
                if t < NT:
                    dve.wait_ge(rstd_done, t + 1)
                    if t >= 2:
                        dve.wait_ge(t_full, 2 * (t - 1))
                    nc.vector.scalar_tensor_tensor(out=hn_s[:, t % 2, :], in0=acc[:, t, :],
                                                   scalar=rstd[:, t:t + 1], in1=g_pre_s[:, :],
                                                   op0=ALU.mult, op1=ALU.mult).then_inc(hn_ready, 1)
                if t:
                    norm_lo(2 * t - 2, t - 1, 0)
                    norm_lo(2 * t - 1, t - 1, 1)
            def qk_lo(hi_count, kind, par, c, b):
                dve.wait_ge(acc_hi, hi_count)
                hi, lo = (q_hi, q_lo) if kind == "q" else (k_hi, k_lo)
                cols = slice(c * HALF, (c + 1) * HALF)
                nc.vector.tensor_tensor(lo[:, par, cols], ACCB[b][:, :], hi[:, par, cols].bitcast(F32),
                                        ALU.subtract).then_inc(acc_free, 1)

            def v_copy(index, c):
                dve.wait_ge(acc_full, index + 1)
                nc.vector.tensor_copy(vT[:, c * HALF:(c + 1) * HALF], ACCB[c][:, :]).then_inc(acc_free, 1)

            for n, (kind, c) in enumerate(FIRST_ACC[:4]):
                qk_lo(n + 1, kind, 0, c, n % 2)
            dve.wait_ge(hn_ready, NT)
            for t in range(NT):
                nc.vector.memset(acc[:, t, :], 0.0)
            v_copy(4, 0)

            def out_add(index, t, c):
                dve.wait_ge(acc_full, index + 1)
                cols = slice(c * HALF, (c + 1) * HALF)
                nc.vector.tensor_tensor(acc[:, t, cols], ACCB[c][:, :], acc[:, t, cols],
                                        ALU.add).then_inc(acc_free, 1)

            def projections(p, par, s, first, proj, tail):
                if s == 0 and not tail:
                    v_copy(acc_base(p) - 1 if not first else 5, 1)
                if proj and s in (4, 8, 20, 24):
                    kind = "q" if s < 16 else "k"
                    c = 0 if s % 8 == 4 else 1
                    qk_lo(4 * p + 4 + (0 if kind == "q" else 2) + c + 1, kind, 1 - par, c, c)
                if proj and s == 28:
                    v_copy(step_units(p, "v")[0], 0)

            def step(p, par, first=False, proj=True, wo=True, slots=SLOTS):
                tail = slots < SLOTS
                for s in range(slots):
                    if s == 8:
                        projections(p, par, s, first, proj and not tail, tail)
                    if not tail and wo and 8 <= s <= 16:
                        index = step_units(p, "wo")[0]
                        if s == 8:
                            dve.wait_ge(acc_free, index)
                        if s > 8:
                            out_add(index + 2 * (s - 9) + 1, s - 9, 1)
                        if s < 16:
                            out_add(index + 2 * (s - 8), s - 8, 0)
                    if s in T_SLOT:
                        n, kind, h, j = T_SLOT[s]
                        g = t_index(p, n)
                        b = n % 2
                        if kind == "v" and not tail:
                            t_lo_sub(g, V[:, j:j + 4, :, 1, :],
                                     TB[b][:, :].rearrange("p (k h c) -> p k h c", k=4, h=2),
                                     V[:, j:j + 4, :, 0, :])
                        elif kind != "v" and not (kind == "prev" and first):
                            w = P * (min(j, 3) + 1 if kind == "lo" else j - 3)
                            t_lo_sub(g, AT_lo[:, b, 0:w], TB[b][:, 0:w], AT_hi[:, b, 0:w])
                    if s != 8:
                        projections(p, par, s, first, proj and not tail, tail)
                    if s in ROW_SLOT and not tail:
                        h, r = ROW_SLOT[s]
                        R = 16 * p + 8 * h + r
                        w = ROW_W[r]
                        st = stay[r % 2]
                        dve.wait_ge(mask_done, R + 1)
                        dve.wait_ge(sig_done, 2 * NCH * p + NCH * h + LAST_CHUNK[r] + 1)
                        nc.vector.tensor_tensor_scan(st[:, 1:1 + w], st[:, 1:1 + w], st[:, 1:1 + w], 1.0,
                                                     ALU.mult, ALU.bypass).then_inc(scan_done, 1)
                        dve.wait_ge(scan_done, R + 1)
                        a = A[r // 4][:, ROW_AT[r]:ROW_AT[r] + w]
                        nc.vector.tensor_tensor(a, a, st[:, 0:w], ALU.mult).then_inc(row_done, 1)
                    if s in O_SLOT and not (first and O_SLOT[s][0] < 0):
                        dp, h, half_q, half = O_SLOT[s]
                        rows = slice(HD * h, HD * (h + 1))
                        dve.wait_ge(o_half, 8 * (p + dp) + 4 * h + 2 * half_q + half + 1)
                        cols = slice(HALF * half_q + 256 * half, HALF * half_q + 256 * half + 256)
                        nc.vector.tensor_tensor(oT_hi[rows, cols], OB[half_q][0:HD, half * 256:half * 256 + 256],
                                                o_part[rows, :], ALU.add)
                        nc.vector.tensor_tensor(o_part[rows, :], OB[half_q][0:HD, half * 256:half * 256 + 256],
                                                o_part[rows, :], ALU.add).then_inc(o_sum, 1)
                        dve.wait_ge(o_sum, 8 * (p + dp) + 4 * h + 2 * half_q + half + 1)
                        nc.vector.tensor_tensor(oT_lo[rows, cols], o_part[rows, :], oT_hi[rows, cols].bitcast(F32),
                                                ALU.subtract).then_inc(o_lo, 1)
                    if tail and s >= 4:
                        norm(s - 4)

            step(0, 0, first=True, wo=False)
            with dve.Fori(0, PAIRS // 2 - 1) as i:
                for u in range(2):
                    step(2 * i + 1 + u, (1 + u) % 2)
            step(PAIRS - 1, 1, proj=False)
            def norm(k):
                if k == 0:
                    dve.wait_ge(gain2_in, 32)
                    dve.wait_ge(acc_free, ACC_END - 16)
                if k < NT:
                    for c in range(2):
                        out_add(ACC_END - 16 + 2 * k + c, k, c)
                if 1 <= k <= NT:
                    t = k - 1
                    dve.wait_ge(rstd_done, NT + (2 * t if t else 1))
                    nc.vector.scalar_tensor_tensor(out=acc[:, t, :], in0=acc[:, t, :],
                                                   scalar=rstd[:, NT + t:NT + t + 1], in1=g_post_t[:, :],
                                                   op0=ALU.mult, op1=ALU.mult).then_inc(mix_scaled, 1)
                if 2 <= k <= NT + 1:
                    t = k - 2
                    dve.wait_ge(rstd_done, NT + 2 * t + 3 if t < NT - 1 else 3 * NT)
                    if t >= 2:
                        dve.wait_ge(t_full, T_TRANS + 2 * (t - 1))
                    nc.vector.scalar_tensor_tensor(out=hn_t[:, t % 2, :], in0=acc[:, t, :],
                                                   scalar=rstd[:, 2 * NT + t:2 * NT + t + 1],
                                                   in1=g_ffn_t[:, :], op0=ALU.mult,
                                                   op1=ALU.mult).then_inc(hn_ready, 1)
                if NORM_LAG <= k:
                    t = k - NORM_LAG
                    for half in range(2):
                        norm_lo(T_TRANS + 2 * t + half, t, half)

            step(PAIRS, 0, proj=False, wo=False, slots=8)
            for k in range(4, NT + NORM_LAG):
                norm(k)

            def ffn_chunk(g, e, par, c):
                n = 4 * g + 2 * e + c
                dve.wait_ge(sg_ready, n + 1)
                gate_b = FIRST_GATE_B[2 * e + c] if isinstance(g, int) and g == 0 else GATEB[c]
                nc.vector.tensor_tensor(sg[:, c, :], gate_b[:, :], sg[:, c, :], ALU.mult).then_inc(silu_ready, 1)
                dve.wait_ge(silu_ready, n + 1)
                nc.vector.tensor_tensor(sg[:, c, :], UPB[c][:, :], sg[:, c, :], ALU.mult).then_inc(prod_ready, 1)

            for e in range(2):
                for c in range(2):
                    ffn_chunk(0, e, 0, c)
            dve.wait_ge(y_zero, 1)

            def y_add(g, k):
                n = 16 * g + k
                dve.wait_ge(y_full, n + 1)
                cols = slice((k % 2) * HALF, (k % 2 + 1) * HALF)
                nc.vector.tensor_tensor(y[:, k // 2, cols], YB[k % 4][:, :], y[:, k // 2, cols],
                                        ALU.add).then_inc(y_free, 1)

            with dve.Fori(0, (NG - 1) // 2) as i:
                for u in range(2):
                    g, par = 2 * i + 1 + u, (1 + u) % 2
                    for c in range(2):
                        ffn_chunk(g, 0, par, c)
                    for c in range(2):
                        ffn_chunk(g, 1, par, c)
                    dve.wait_ge(prod_ready, 4 * g + 4)
                    for k in range(16):
                        y_add(g - 1, k)

            dve.wait_ge(y_free, 16 * (NG - 1))
            dve.wait_ge(gain3_in, 16)

            def finish(t):
                dve.wait_ge(rstd_done, 3 * NT + t + 1)
                nc.vector.scalar_tensor_tensor(out=y[:, t, :], in0=y[:, t, :], scalar=rstd[:, t:t + 1],
                                               in1=g_out[:, :], op0=ALU.mult, op1=ALU.mult).then_inc(y_scaled, 1)
                dve.wait_ge(y_scaled, t + 1)
                nc.vector.tensor_tensor(y[:, t, :], y[:, t, :], acc[:, t, :], ALU.add).then_inc(out_ready, 1)

            for t in range(NT + 1):
                if t < NT:
                    y_add(NG - 1, 2 * t)
                    y_add(NG - 1, 2 * t + 1)
                if t:
                    finish(t - 1)

        @block.tensor
        def _(pe):
            def project_tiles(c, slot, kts, b):
                for kt in kts:
                    wh = w_hi[slot][:, kt * P:(kt + 1) * P]
                    wl = w_lo[slot][:, kt * P:(kt + 1) * P]
                    cols = slice(c * HALF, (c + 1) * HALF)
                    nc.tensor.matmul(ACCB[b][:, :], wh, hnT_hi[:, kt, cols], start=(kt == 0), stop=False)
                    nc.tensor.matmul(ACCB[b][:, :], wh, hnT_lo[:, kt, cols], start=False, stop=False)
                    mm = nc.tensor.matmul(ACCB[b][:, :], wl, hnT_hi[:, kt, cols], start=False, stop=(kt == KT - 1))
                if kts[-1] == KT - 1:
                    mm.then_inc(acc_full, 1)

            def transpose_norm(n, src, half):
                if n >= 2:
                    pe.wait_ge(t_lo, n - 1)
                for q in range(4):
                    k = 4 * half + q
                    mm = nc.tensor.transpose(TB[n % 2][:, q * P:(q + 1) * P], src[:, k * P:(k + 1) * P], ident[:, :])
                mm.then_inc(t_full, 1)

            pe.wait_ge(consts, 7)
            for t in range(NT + 1):
                if t < NT:
                    pe.wait_ge(hn_ready, t + 1)
                    for half in range(2):
                        transpose_norm(2 * t + half, hn_s[:, t % 2, :], half)
                for n in {4: [0], 6: [1], NT: [2, 3, 4, 5]}.get(t, []):
                    kind, c = FIRST_ACC[n]
                    unit = "qkv".index(kind)
                    pe.wait_ge(w_ready, unit + 1)
                    pe.wait_ge(t_lo, NT * (c + 1))
                    if n >= 2:
                        pe.wait_ge(acc_free, n - 1)
                    project_tiles(c, unit % 2, range(KT), n % 2)

            def out_project(index, t, c, slot):
                pe.wait_ge(acc_free, index + c - 1)
                cols = slice(c * HALF, (c + 1) * HALF)
                oh, ol = oT_hi[:, t * P:(t + 1) * P], oT_lo[:, t * P:(t + 1) * P]
                nc.tensor.matmul(ACCB[c][:, :], oh, w_hi[slot][:, cols], start=True, stop=False)
                nc.tensor.matmul(ACCB[c][:, :], oh, w_lo[slot][:, cols], start=False, stop=False)
                nc.tensor.matmul(ACCB[c][:, :], ol, w_hi[slot][:, cols], start=False, stop=True
                                 ).then_inc(acc_full, 1)

            def out_last(k, c):
                if k == 0 and c == 0:
                    pe.wait_ge(w_ready, UNITS1)
                    pe.wait_ge(o_lo, 8 * PAIRS - 2)
                if k == 4 and c == 0:
                    pe.wait_ge(o_lo, 8 * PAIRS)
                out_project(ACC_END - 16 + 2 * k, k, c, 1)

            def fill(p, s, part, proj, wo):
                kind = FILL_KIND[s // 8]
                if kind == "wo":
                    if wo:
                        index, n = step_units(p, "wo")
                        if s == 8 and part == 0:
                            pe.wait_ge(w_ready, n + 1)
                            pe.wait_ge(o_lo, 8 * p - 2)
                        if s == 12 and part == 0:
                            pe.wait_ge(o_lo, 8 * p)
                        out_project(index + 2 * (s - 8), s - 8, part, unit_slot(p, "wo"))
                elif proj:
                    index, n = step_units(p, kind)
                    c = (s % 8) // 4
                    if part == 0:
                        if s % 8 == 0:
                            pe.wait_ge(w_ready, n + 1)
                        if s % 4 == 0:
                            pe.wait_ge(acc_free, index + c - 1)
                    k0 = 2 * (s % 4) + part
                    project_tiles(c, unit_slot(p, kind), range(k0, k0 + 1), c)

            def step(p, par, first=False, proj=True, wo=True, slots=SLOTS):
                tail = slots < SLOTS
                for s in range(slots):
                    dp = 0
                    at = s - AV_LAG
                    if at < 0:
                        dp, at = -1, at + SLOTS
                    if at in T_SLOT and T_SLOT[at][1] != "v" and not (first and (dp < 0 or T_SLOT[at][1] == "prev")):
                        n, kind, h, j = T_SLOT[at]
                        half_q = 0 if kind == "lo" else 1
                        start = j == (0 if kind == "lo" else 4)
                        stop = j == NT - 1
                        w = P * (min(j, 3) + 1 if kind == "lo" else j - 3)
                        b = n % 2
                        if start:
                            sb = 4 * (p + dp) + 2 * h + half_q - (4 if kind == "prev" else 0)
                            if not (isinstance(sb, int) and sb < 2):
                                pe.wait_ge(o_sum, 2 * (sb - 1))
                        pe.wait_ge(t_lo, t_index(p + dp, n) + 1)
                        v = V[:, j, h, :, :].rearrange("p a c -> p (a c)")
                        nc.tensor.matmul(OB[half_q][:, 0:w], v, AT_hi[:, b, 0:w], start=start, stop=False,
                                         skip_group_check=True)
                        nc.tensor.matmul(OB[half_q][:, 0:w], v, AT_lo[:, b, 0:w], start=False, stop=stop,
                                         skip_group_check=True).then_inc(av_done, 1)
                    if not tail:
                        fill(p, s, 0, proj, wo)
                    elif s >= 4:
                        out_last(s - 4, 0)
                    if s in T_SLOT:
                        n, kind, h, j = T_SLOT[s]
                        g = t_index(p, n)
                        b = n % 2
                        if kind == "v" and not tail:
                            pe.wait_ge(t_lo, g - 1)
                            if n == 4:
                                pe.wait_ge(acc_free, acc_base(p) if not first else 6)
                            for q in range(4):
                                mm = nc.tensor.transpose(TB[b][:, q * P:(q + 1) * P],
                                                         vT[:, (j + q) * P:(j + q + 1) * P], ident[:, :])
                            mm.then_inc(t_full, 1)
                        elif kind != "v" and not (kind == "prev" and first):
                            pe.wait_ge(t_lo, g - 1)
                            rows = range(0, min(j, 3) + 1) if kind == "lo" else range(4, j + 1)
                            hp = 16 * p + 8 * h - (16 if kind == "prev" else 0)
                            pe.wait_ge(row_done, hp + rows[-1] + 1)
                            for q, r in enumerate(rows):
                                at_ = ROW_AT[r] + (j - r) * P
                                mm = nc.tensor.transpose(TB[b][:, q * P:(q + 1) * P],
                                                         A[r // 4][:, at_:at_ + P], ident[:, :])
                            mm.then_inc(t_full, 1)
                    if s in Z_SLOT and not tail:
                        h, c = Z_SLOT[s]
                        r, a, e, _ = CHUNKS[c]
                        z = 2 * NCH * p + NCH * h + c
                        if s == 0:
                            pe.wait_ge(acc_free, 4 if first else acc_base(p) - 2)
                        if not (isinstance(z, int) and z < 2):
                            pe.wait_ge(sig_done, z - 1)
                        hr = slice(HD * h, HD * (h + 1))
                        qs, ks = slice(r * P, (r + 1) * P), slice(a, e)
                        dst = ZB[c % 2][:, 0:e - a]
                        nc.tensor.matmul(dst, q_hi[hr, par, qs], k_hi[hr, par, ks], start=True, stop=False)
                        nc.tensor.matmul(dst, q_hi[hr, par, qs], k_lo[hr, par, ks], start=False, stop=False)
                        nc.tensor.matmul(dst, q_lo[hr, par, qs], k_hi[hr, par, ks], start=False, stop=True
                                         ).then_inc(z_full, 1)
                    if not tail:
                        fill(p, s, 1, proj, wo)
                    elif s >= 4:
                        out_last(s - 4, 1)
                        if s == 7:
                            pe.wait_ge(hn_ready, NT + 1)
                            for half in range(2):
                                transpose_norm(T_TRANS + half, hn_t[:, 0, :], half)

            step(0, 0, first=True, wo=False)
            with pe.Fori(0, PAIRS // 2 - 1) as i:
                for u in range(2):
                    step(2 * i + 1 + u, (1 + u) % 2)
            step(PAIRS - 1, 1, proj=False)
            step(PAIRS, 0, proj=False, wo=False, slots=8)

            def gate_up(is_up, c, slot, bank_ap):
                cols = slice(c * HALF, (c + 1) * HALF)
                for kt in range(KT):
                    wh = w_hi[slot][:, kt * P:(kt + 1) * P]
                    wl = w_lo[slot][:, kt * P:(kt + 1) * P]
                    nc.tensor.matmul(bank_ap, wh, hnT_hi[:, kt, cols], start=(kt == 0), stop=False)
                    nc.tensor.matmul(bank_ap, wh, hnT_lo[:, kt, cols], start=False, stop=False)
                    mm = nc.tensor.matmul(bank_ap, wl, hnT_hi[:, kt, cols], start=False, stop=(kt == KT - 1))
                mm.then_inc(up_full if is_up else gate_full, 1)

            def gate_up_first(m, c):
                pe.wait_ge(w_ready, UNITS1 + m + 1)
                if m % 2 == 0:
                    dst = FIRST_GATE_B[m + c]
                else:
                    dst = UPB[c]
                    if m == 3:
                        pe.wait_ge(prod_ready, c + 1)
                gate_up(m % 2 == 1, c, m % 3, dst[:, :])

            for k in range(4, NT + NORM_LAG):
                if k < NT:
                    for c in range(2):
                        out_last(k, c)
                if k == NT - 1:
                    pe.wait_ge(t_lo, T_TRANS + NT)
                if NT - 1 <= k < NT + 2:
                    gate_up_first(k - (NT - 1), 0)
                t = k - NORM_LAG
                pe.wait_ge(hn_ready, NT + t + 1)
                for half in range(2):
                    transpose_norm(T_TRANS + 2 * t + half, hn_t[:, t % 2, :], half)
            def down(g, par, slots, last=False):
                pe.wait_ge(h_ready, 4 * g + 4)
                for k in range(16):
                    t, c = k // 2, k % 2
                    cols = slice(c * HALF, (c + 1) * HALF)
                    if k >= 4 or last:
                        pe.wait_ge(y_free, 16 * g + k - 3)
                    for e in range(2):
                        hh = h_hi[:, par, e, t * P:(t + 1) * P]
                        hl = h_lo[:, par, e, t * P:(t + 1) * P]
                        wh, wl = w_hi[slots[e]][:, cols], w_lo[slots[e]][:, cols]
                        nc.tensor.matmul(YB[k % 4][:, :], hh, wh, start=(e == 0), stop=False)
                        nc.tensor.matmul(YB[k % 4][:, :], hh, wl, start=False, stop=False)
                        mm = nc.tensor.matmul(YB[k % 4][:, :], hl, wh, start=False, stop=(e == 1))
                    mm.then_inc(y_full, 1)

            pe.wait_ge(t_lo, T_END)
            for m, c in ((0, 1), (1, 1), (2, 1), (3, 0), (3, 1)):
                gate_up_first(m, c)

            with pe.Fori(0, (NG - 1) // 2) as i:
                for u in range(2):
                    g, par, m_mod = 2 * i + 1 + u, (1 + u) % 2, (4 + 6 * u) % 3
                    base = UNITS1 + 6 * g - 2
                    for m in range(4):
                        pe.wait_ge(w_ready, base + m + 1)
                        for c in range(2):
                            n = 4 * g + 2 * (m // 2) + c
                            if m % 2 == 0:
                                pe.wait_ge(prod_ready, n - 1)
                            gate_up(m % 2 == 1, c, (m_mod + m) % 3, (UPB if m % 2 else GATEB)[c][:, :])
                    pe.wait_ge(w_ready, base + 6)
                    down(g - 1, 1 - par, [(m_mod + 4) % 3, (m_mod + 5) % 3])
            pe.wait_ge(w_ready, UNITS)
            m = 6 * (NG - 1) + 4
            down(NG - 1, (NG - 1) % 2, [m % 3, (m + 1) % 3], last=True)


def kernel(**inputs):
    import numpy as _np
    import concourse.bacc as _bacc
    from concourse import mybir as _mybir
    from concourse.bass_utils import run_bass_kernel_spmd as _run

    a = {k: _np.asarray(v) for k, v in inputs.items()}

    def col_units(w, n):
        return w[:, n * P:(n + 1) * P].reshape(KT, P, P).transpose(1, 0, 2).reshape(P, D)

    w_qkv, w_o, w_gu, w_down = a["sb_w_qkv"][0], a["sb_w_o"][0], a["ffn_w_gu"][0], a["ffn_w_down"][0]
    q = [col_units(w_qkv, p) for p in range(PAIRS)]
    k = [col_units(w_qkv, PAIRS + p) for p in range(PAIRS)]
    v = [col_units(w_qkv, 2 * PAIRS + p) for p in range(PAIRS)]
    wo = [w_o[p * P:(p + 1) * P] for p in range(PAIRS)]
    gate = [col_units(w_gu, f) for f in range(NF)]
    up = [col_units(w_gu, NF + f) for f in range(NF)]
    down = [w_down[f * P:(f + 1) * P] for f in range(NF)]
    order = [q[0], k[0], v[0], q[1], k[1], v[1]]
    for p in range(1, PAIRS - 1):
        order += [q[p + 1], wo[p - 1], k[p + 1], v[p + 1]]
    order += [wo[PAIRS - 2], wo[PAIRS - 1], gate[0], up[0], gate[1], up[1]]
    for g in range(1, NG):
        order += [gate[2 * g], up[2 * g], gate[2 * g + 1], up[2 * g + 1], down[2 * g - 2], down[2 * g - 1]]
    order += [down[NF - 2], down[NF - 1]]

    arrays = {
        "in_x": _np.ascontiguousarray(a["x"][:, ::-1]),
        "in_mix_pre": _np.ascontiguousarray(a["ln_mix_pre"][0]),
        "in_mix_post": _np.ascontiguousarray(a["ln_mix_post"][0]),
        "in_ffn_pre": _np.ascontiguousarray(a["ln_ffn_pre"][0]),
        "in_ffn_post": _np.ascontiguousarray(a["ln_ffn_post"][0]),
        "in_units": _np.ascontiguousarray(_np.stack(order)),
    }
    nc = _bacc.Bacc("TRN2", target_bir_lowering=False, num_devices=1)
    args = [nc.dram_tensor(n, t.shape, _mybir.dt.from_np(t.dtype), kind="ExternalInput").ap()
            for n, t in arrays.items()]
    args.append(nc.dram_tensor("out_0", a["x"].shape, _mybir.dt.float32, kind="ExternalOutput").ap())
    encoder_layer(nc, *args)
    r = _run(nc, [arrays], core_ids=[0])
    return _np.ascontiguousarray(_np.asarray(r.results[0]["out_0"])[:, ::-1])
```

```python
from contextlib import ExitStack

import concourse.bass as bass
from concourse import mybir

F32 = mybir.dt.float32
F32R = mybir.dt.float32r
ALU = mybir.AluOpType
ACT = mybir.ActivationFunctionType

P = 128
D = 1024
SEQ = 1024
KT = D // P
NT = SEQ // P
HALF = 512
HD = 64
PAIRS = D // (2 * HD)
D_FF = ((8 * D + 3 * 256 - 1) // (3 * 256)) * 256
NF = D_FF // P
NG = NF // 2
Z_SCALE = HD ** -0.5
EPS = 1e-6
UNITS1 = 4 * PAIRS
UNITS = UNITS1 + 3 * NF
SLOTS = 32

ROW_W = [SEQ - P * r for r in range(NT)]
ROW_AT = [sum(ROW_W[:r]) if r < 4 else sum(ROW_W[4:r]) for r in range(NT)]
A_SIZE = [sum(ROW_W[:4]), sum(ROW_W[4:])]


def row_chunks(r):
    return [(P * r, HALF), (HALF, SEQ)] if r < 4 else [(P * r, SEQ)]


CHUNKS = [(r, a, b, n == len(row_chunks(r)) - 1) for r in range(NT) for n, (a, b) in enumerate(row_chunks(r))]
NCH = len(CHUNKS)
LAST_CHUNK = [max(n for n, c in enumerate(CHUNKS) if c[0] == r) for r in range(NT)]

def z_slot(h, c):
    return 16 * h + (c if c < 8 else 8 + 2 * (c - 8))


Z_SLOT = {z_slot(h, c): (h, c) for h in range(2) for c in range(NCH)}
ROW_SLOT = {z_slot(h, LAST_CHUNK[r]) + 1: (h, r) for h in range(2) for r in range(NT)}
T_SLOT = {}
for _n, _s in enumerate((0, 1, 2, 3)):
    T_SLOT[_s] = [(_n, "prev", 1, 4 + _n)]
for _n, _s in enumerate((6, 8)):
    T_SLOT[_s] = [(4 + _n, "v", 0, 4 * _n)]
for _n in range(8):
    T_SLOT.setdefault(8 + _n, []).append((6 + _n, "lo", 0, _n))
    T_SLOT[24 + _n] = [(18 + _n, "lo", 1, _n)]
for _n, _s in enumerate((16, 18, 20, 22)):
    T_SLOT[_s] = [(14 + _n, "up", 0, 4 + _n)]
POOL_ROWS = [(0, r) for r in range(5, NT)]
AFTER_POOL_ROWS = (1, 0)
T_PER_STEP = 26
T_START = 2 * NT
AV_LAG = 2


def t_index(p, n):
    return T_START - 4 + T_PER_STEP * p + n


def av_index(p, kind, h, j):
    if kind == "prev":
        return 2 * NCH * p - 4 + (j - 4)
    return 2 * NCH * p + NCH * h + (j if kind == "lo" else 8 + j - 4)


ACC_OFF = {"v": 0, "wo": 2, "k": 18, "q": 20}
UNIT_OFF = {"v": 0, "wo": 1, "k": 2, "q": 3}
FILL_KIND = ["v", "wo", "k", "q"]


def acc_base(p):
    return 4 if isinstance(p, int) and p == 0 else 10 + 22 * (p - 1)


def unit_base(p):
    return 2 if isinstance(p, int) and p == 0 else 5 + 4 * (p - 1)


def step_units(p, kind):
    if isinstance(p, int) and p == 0:
        n = {"v": 0, "k": 1, "q": 2}[kind]
        return 4 + 2 * n, 2 + n
    if isinstance(p, int) and p == PAIRS:
        return acc_base(PAIRS - 1) + 18, unit_base(PAIRS - 1) + 2
    return acc_base(p) + ACC_OFF[kind], unit_base(p) + UNIT_OFF[kind]


def unit_parity(p, kind):
    return step_units(p, kind)[1] % 2 if isinstance(p, int) else (UNIT_OFF[kind] + 1) % 2


ACC_END = acc_base(PAIRS - 1) + 2 + 32
T_TRANS = T_START - 4 + T_PER_STEP * PAIRS + 4
T_END = T_TRANS + 2 * NT


def has_unit(p, s):
    if isinstance(p, int) and p == 0:
        return s // 8 != 1
    return s // 8 < 2 if isinstance(p, int) and p == PAIRS - 1 else True


O_SLOT = {2: [(-1, 1, 0, 0)], 3: [(-1, 1, 0, 1)], 6: [(-1, 1, 1, 0)], 7: [(-1, 1, 1, 1)],
          18: [(0, 0, 0, 0)], 19: [(0, 0, 0, 1)], 25: [(0, 0, 1, 0)], 26: [(0, 0, 1, 1)]}
TAIL_O_SLOT = {1: [(-1, 1, 0, 0), (-1, 1, 0, 1)], 5: [(-1, 1, 1, 0), (-1, 1, 1, 1)]}
TAIL, TAIL_SLOTS = 2, 6


def value_halves(s, first, tail):
    return [o for o in (TAIL_O_SLOT if tail else O_SLOT).get(s, []) if not (first and o[0] < 0)]


FIRST_ACC = [("k", 0), ("q", 0), ("k", 1), ("q", 1)]
FIRST_PARTS = {3: [(0, range(0, 2))], 4: [(0, range(2, KT))], 6: [(1, range(0, 5))],
               7: [(1, range(5, KT))],
               NT: [(2, range(KT)), (3, range(KT))]}
NORM = [(0, None, None, None),
        (1, 0, None, None),
        (2, 1, None, None),
        (3, 2, 0, None),
        (None, 3, 1, 0),
        (4, None, 2, 1),
        (5, 4, 3, 2),
        (6, 5, None, 3),
        (7, 6, 4, None),
        (None, 7, 5, 4),
        (None, None, 6, 5),
        (None, None, 7, 6),
        (None, None, None, 7)]
NORM_IN_TAIL = TAIL_SLOTS - TAIL
SQUARES = []
for _i, _row in enumerate(NORM):
    SQUARES += [("mix", _row[0])] * (_row[0] is not None)
    SQUARES += [("x2", NORM[_i - 1][1])] * (_i > 0 and NORM[_i - 1][1] is not None)
FIRST_SPLITS = {5: 1, 8: 2}
FIRST_CHUNKS = {7: 0, 8: 1, 9: 2}


def ring(m):
    return (0, 2, 1)[m % 3]


def square_index(kind, t):
    return NT + SQUARES.index((kind, t))


def encoder_layer(nc, x, g_mix_pre, g_mix_post, g_ffn_pre, g_ffn_post, units, out):
    ctx = ExitStack()
    with ctx:
        def sem(name):
            return ctx.enter_context(nc.semaphore(name))

        def alloc(stack, name, shape, dt=F32):
            return stack.enter_context(nc.sbuf_tensor(name, shape, dt))

        hnT_hi = alloc(ctx, "hnT_hi", [P, KT, SEQ], F32R)
        hnT_lo = alloc(ctx, "hnT_lo", [P, KT, SEQ], F32R)
        acc = alloc(ctx, "acc", [P, NT, D])
        raw = alloc(ctx, "raw", [P, 2, D])
        w_hi01 = alloc(ctx, "w_hi01", [P, 2, D], F32R)
        w_lo01 = alloc(ctx, "w_lo01", [P, 2, D], F32R)
        ident = alloc(ctx, "ident", [P, P])
        keep = alloc(ctx, "keep", [P, P], mybir.dt.bfloat16)
        ss = alloc(ctx, "ss", [P, 4 * NT])
        ms = alloc(ctx, "ms", [P, 3 * NT])
        rstd = alloc(ctx, "rstd", [P, 3 * NT])
        mhalf = alloc(ctx, "mhalf", [P, 1])

        with ExitStack() as one:
            A = [alloc(one, f"A{n}", [P, A_SIZE[n]]) for n in range(2)]
            with ExitStack() as qk:
                q_hi2 = alloc(qk, "q_hi2", [P, 2, SEQ], F32R)
                q_lo = alloc(qk, "q_lo", [P, SEQ], F32R)
                k_a = alloc(qk, "k_a", [P, SEQ], F32R)
                k_b = alloc(qk, "k_b", [P, 2, SEQ], F32R)
                vT = alloc(qk, "vT", [P, SEQ])
                V = alloc(qk, "V", [P, NT, 2, 2, HD], F32R)
                stay = [alloc(qk, "stay0", [P, 1 + SEQ]), alloc(qk, "stay1", [P, 1 + SEQ - P])]
                AT_hi = alloc(qk, "AT_hi", [P, 2, HALF], F32R)
                AT_lo = alloc(qk, "AT_lo", [P, 2, HALF], F32R)
                oT_hi = alloc(qk, "oT_hi", [P, SEQ], F32R)
                oT_lo = alloc(qk, "oT_lo", [P, SEQ], F32R)
                o_part = alloc(qk, "o_part", [P, 2, HALF // 2])
            with ExitStack() as tr:
                g_post_t = alloc(tr, "g_post_t", [P, D])
                g_ffn_t = alloc(tr, "g_ffn_t", [P, D])
                x_in = alloc(tr, "x_in", [P, 2, D])
                hn_t = alloc(tr, "hn_t", [P, 2, D])
                junk_t = alloc(tr, "junk_t", [P, D])
        with ExitStack() as st:
            g_pre_s = alloc(st, "g_pre_s", [P, D])
            hn_s = alloc(st, "hn_s", [P, 2, D])
            junk_s = alloc(st, "junk_s", [P, D])
        with ExitStack() as two:
            w_hi2 = alloc(two, "w_hi2", [P, D], F32R)
            w_lo2 = alloc(two, "w_lo2", [P, D], F32R)
            g_out = alloc(two, "g_out", [P, D])
            sg = alloc(two, "sg", [P, 2, HALF])
            alloc(two, "gap", [P, sum(A_SIZE) - 4 * D])
            y = alloc(two, "y", [P, NT, D])
            h_hi = alloc(two, "h_hi", [P, 2, 2, SEQ], F32R)
            h_lo = alloc(two, "h_lo", [P, 2, 2, SEQ], F32R)

        bank = [ctx.enter_context(nc.psum_tensor(f"bank{n}", [P, HALF], F32)) for n in range(8)]
        ACCB = bank[0:2]
        ZB = bank[2:4]
        TB = bank[4:6]
        OB = bank[6:8]
        FIRST_ACC_B = ACCB + OB
        GATEB, UPB = ZB, OB
        YB = ACCB + TB
        FIRST_GATE_B = [ZB[0], ACCB[0], ZB[1], ACCB[1]]

        OWN = [slice(0, HD), slice(HD, P)]
        OTHER = [OWN[1], OWN[0]]

        def k_tile(h, par):
            return k_b[:, par, :] if h else k_a[:, :]

        w_hi = [w_hi01[:, 0, :], w_hi01[:, 1, :], w_hi2[:, :], hnT_hi[:, 0, :]]
        w_lo = [w_lo01[:, 0, :], w_lo01[:, 1, :], w_lo2[:, :], hnT_lo[:, 0, :]]
        LAST_SLOT = 3

        x_tile = [sem(f"x_tile{t}") for t in range(NT)]
        raw_in = [sem("raw_in0"), sem("raw_in1")]
        gain_in = sem("gain_in")
        gain2_in = sem("gain2_in")
        gain3_in = sem("gain3_in")
        x_again = [sem("x_again0"), sem("x_again1")]
        out_done = sem("out_done")
        consts = sem("consts")
        w_hi_ready = sem("w_hi_ready")
        w_ready = sem("w_ready")
        sq_done = sem("sq_done")
        ms_done = sem("ms_done")
        rstd_done = sem("rstd_done")
        hn_ready = sem("hn_ready")
        mix_scaled = sem("mix_scaled")
        x2_ready = sem("x2_ready")
        t_full = sem("t_full")
        t_hi = sem("t_hi")
        t_lo = sem("t_lo")
        acc_full = sem("acc_full")
        acc_hi = sem("acc_hi")
        acc_free = sem("acc_free")
        z_full = sem("z_full")
        sig_done = sem("sig_done")
        mask_done = sem("mask_done")
        scan_done = sem("scan_done")
        row_done = sem("row_done")
        av_done = sem("av_done")
        o_half = sem("o_half")
        o_sum = sem("o_sum")
        o_hi = sem("o_hi")
        o_lo = sem("o_lo")
        gate_full = sem("gate_full")
        up_full = sem("up_full")
        sg_ready = sem("sg_ready")
        silu_ready = sem("silu_ready")
        prod_ready = sem("prod_ready")
        h_hi_ready = sem("h_hi_ready")
        h_ready = sem("h_ready")
        y_zero = sem("y_zero")
        y_full = sem("y_full")
        y_free = sem("y_free")
        ysq_done = sem("ysq_done")
        y_scaled = sem("y_scaled")
        even_out = sem("even_out")
        odd_out = sem("odd_out")

        x_tiles = x.rearrange("b (t p) d -> p (b t) d", p=P)
        out_tiles = out.rearrange("b (t p) d -> p (b t) d", p=P)

        block = ctx.enter_context(nc.Block())

        @block.sync
        def _(sp):
            for t in range(4):
                sp.dma_start(acc[:, t, :], x_tiles[:, t, :]).then_inc(x_tile[t], 16)
            sp.dma_start(raw[:, 0, :], units[0]).then_inc(raw_in[0], 16)
            for t in range(4, NT):
                sp.dma_start(acc[:, t, :], x_tiles[:, t, :]).then_inc(x_tile[t], 16)
            sp.dma_start(raw[:, 1, :], units[1]).then_inc(raw_in[1], 16)
            with sp.Fori(1, UNITS // 2) as i:
                for s in range(2):
                    sp.wait_ge(w_ready, 2 * i + s - 1)
                    sp.dma_start(raw[:, s, :], units[bass.ds(2 * i + s, 1)].rearrange("a p n -> p (a n)")
                                 ).then_inc(raw_in[s], 16)
            for t in range(NT - 1):
                sp.wait_ge(odd_out if t % 2 else even_out, t // 2 + 1)
                sp.dma_start(out_tiles[:, t, :], y[:, t, :]).then_inc(out_done, 16)
            for c in range(2):
                sp.wait_ge(odd_out, NT // 2 + c)
                cols = slice(c * HALF, (c + 1) * HALF)
                sp.dma_start(out_tiles[:, NT - 1, cols], y[:, NT - 1, cols]).then_inc(out_done, 16)
            sp.wait_ge(out_done, 16 * (NT + 1))

        @block.scalar
        def _(act):
            def split_hi(n, slot, raw_slot, count):
                act.wait_ge(raw_in[raw_slot], count)
                nc.scalar.activation(w_hi[slot], raw[:, raw_slot, :], ACT.Copy).then_inc(w_hi_ready, 1)

            def raw_count(n, parity):
                return 16 * (n // 2 + 1) if isinstance(n, int) else 8 * (n - parity) + 16

            def t_hi_copy(index, out_ap, in_ap):
                act.wait_ge(t_full, index + 1)
                nc.scalar.activation(out_ap, in_ap, ACT.Copy).then_inc(t_hi, 1)

            act.dma_start(g_pre_s[:, :], g_mix_pre.partition_broadcast(P)).then_inc(gain_in, 16)

            def start_hi(t):
                for half in range(2):
                    n = 2 * t + half
                    t_hi_copy(n, hnT_hi[:, 4 * half:4 * half + 4, t * P:(t + 1) * P],
                              TB[n % 2][:, :].rearrange("p (k c) -> p k c", k=4))

            for t in range(NT):
                act.wait_ge(x_tile[t], 16)
                if t:
                    act.wait_ge(sq_done, t)
                nc.scalar.activation(junk_s[:, :], acc[:, t, :], ACT.Square,
                                     accum_out=ss[:, t:t + 1]).then_inc(sq_done, 1)
                if t == 3:
                    split_hi(0, 0, 0, 16)
                if t == 6:
                    split_hi(1, 1, 1, 16)
                if t >= 2:
                    start_hi(t - 2)
            start_hi(NT - 2)
            start_hi(NT - 1)

            def qk_hi(index, kind, par, c, src):
                act.wait_ge(acc_full, index + 1)
                cols = slice(c * HALF, (c + 1) * HALF)
                for h in range(2):
                    dst = q_hi2[:, h, :] if kind == "q" else k_tile(h, par)
                    copy = nc.scalar.activation(dst[OWN[h], cols], src[OWN[h], :], ACT.Copy)
                    if kind == "q":
                        copy = nc.scalar.activation(dst[OTHER[h], cols], src[OWN[h], :], ACT.Copy)
                copy.then_inc(acc_hi, 1)

            for n, (kind, c) in enumerate(FIRST_ACC):
                qk_hi(n, kind, 0, c, FIRST_ACC_B[n])
                if n == 2:
                    split_hi(2, 0, 0, raw_count(2, 0))

            def split_next(p, kind):
                index, n = step_units(p, kind)
                par = 1 - unit_parity(p, kind)
                act.wait_ge(acc_full, index)
                split_hi(n + 1, par, par, raw_count(n + 1, par))

            def o_copy(p, dp, h, half_q, half):
                sb = 4 * (p + dp) + 2 * h + half_q
                act.wait_ge(av_done, 2 * NCH * (p + dp) + NCH * h + (NCH if half_q else 8))
                if not (isinstance(sb, int) and sb == 0):
                    act.wait_ge(o_lo, 2 * sb + half - 1)
                nc.scalar.activation(o_part[OWN[h], half, :], OB[half_q][HD:P, half * 256:half * 256 + 256],
                                     ACT.Copy).then_inc(o_half, 1)

            def o_hi_copy(p, dp, h, half_q, half):
                act.wait_ge(o_sum, 8 * (p + dp) + 4 * h + 2 * half_q + half + 1)
                cols = slice(HALF * half_q + 256 * half, HALF * half_q + 256 * half + 256)
                nc.scalar.activation(oT_hi[OWN[h], cols], o_part[OWN[h], half, :], ACT.Copy).then_inc(o_hi, 1)

            def step(p, par, first=False, proj=True, wo=True, slots=SLOTS):
                tail = slots < SLOTS
                for s in range(slots):
                    if s in (4, 8) and not tail:
                        c = s // 8
                        act.wait_ge(acc_full, acc_base(p) + c + 1)
                        act.wait_ge(acc_free, acc_base(p) + c)
                        nc.scalar.activation(vT[:, c * HALF:(c + 1) * HALF], ACCB[c][:, :],
                                             ACT.Copy).then_inc(acc_free, 1)
                    for n, kind, h, j in T_SLOT.get(s, []):
                        g = t_index(p, n)
                        b = n % 2
                        if kind == "v" and not tail:
                            if not first:
                                act.wait_ge(av_done, 2 * NCH * p)
                            t_hi_copy(g, V[:, j:j + 4, :, 0, :],
                                      TB[b][:, :].rearrange("p (k h c) -> p k h c", k=4, h=2))
                        elif kind != "v" and not (kind == "prev" and first):
                            a = av_index(p, kind, h, j)
                            if not (isinstance(a, int) and a < 2):
                                act.wait_ge(av_done, a - 1)
                            w = P * (min(j, 3) + 1 if kind == "lo" else j - 3)
                            t_hi_copy(g, AT_hi[:, b, 0:w], TB[b][:, 0:w])
                    if s in Z_SLOT and not tail:
                        h, c = Z_SLOT[s]
                        r, a, e, _ = CHUNKS[c]
                        z = 2 * NCH * p + NCH * h + c
                        R = 16 * p + 8 * h + r
                        if (c == 0 or CHUNKS[c - 1][0] != r) and not (isinstance(R, int) and R < 2):
                            act.wait_ge(row_done, R - 1)
                        act.wait_ge(z_full, z + 1)
                        at = ROW_AT[r] + a - P * r
                        nc.scalar.activation(A[r // 4][:, at:at + e - a], ZB[c % 2][:, 0:e - a],
                                             ACT.Sigmoid, scale=Z_SCALE)
                        nc.scalar.activation(stay[r % 2][:, 1 + a - P * r:1 + e - P * r], ZB[c % 2][:, 0:e - a],
                                             ACT.Sigmoid, scale=-Z_SCALE).then_inc(sig_done, 1)
                    if s == 0 and not first and not tail:
                        qk_hi(acc_base(p) - 1, "q", par, 1, ACCB[1])
                    if proj and s in (20, 24) and not tail:
                        qk_hi(step_units(p, "k")[0] + s // 24, "k", 1 - par, s // 24, ACCB[s // 24])
                    if proj and s == 28 and not tail:
                        qk_hi(step_units(p, "q")[0], "q", 1 - par, 0, ACCB[0])
                    if not tail:
                        for o in value_halves(s - 1, first, tail):
                            o_hi_copy(p, *o)
                    for o in value_halves(s, first, tail):
                        o_copy(p, *o)
                    if tail:
                        if s > TAIL:
                            norm_x2(s - TAIL - 1)
                        for o in value_halves(s, first, tail):
                            o_hi_copy(p, *o)
                    if s % 8 == 1 and not tail and has_unit(p, s):
                        split_next(p, FILL_KIND[s // 8])
                    if tail and s >= TAIL:
                        norm(s - TAIL)

            step(0, 0, first=True, wo=False)
            with act.Fori(0, PAIRS // 2 - 1) as i:
                for u in range(2):
                    step(2 * i + 1 + u, (1 + u) % 2)
            step(PAIRS - 1, 1, proj=False)

            def split_at(m, waits):
                for s, v in waits:
                    act.wait_ge(s, v)
                split_hi(UNITS1 + m, ring(m), m % 2, 16 * ((UNITS1 + m) // 2 + 1))

            def square(kind, t, col):
                act.wait_ge(sq_done, square_index(kind, t))
                nc.scalar.activation(junk_t[:, :], acc[:, t, :], ACT.Square,
                                     accum_out=ss[:, col:col + 1]).then_inc(sq_done, 1)

            def norm(i):
                add, _, _, split = NORM[i]
                if split is not None:
                    for half in range(2):
                        n = T_TRANS + 2 * split + half
                        t_hi_copy(n, hnT_hi[:, 4 * half:4 * half + 4, split * P:(split + 1) * P],
                                  TB[n % 2][:, :].rearrange("p (k c) -> p k c", k=4))
                if add is not None:
                    act.wait_ge(acc_free, ACC_END - 16 + 2 * (add + 1))
                    square("mix", add, NT + add)

            def norm_x2(i):
                t = NORM[i - 1][1] if i else None
                if t is not None:
                    act.wait_ge(x2_ready, t + 1)
                    if t + 2 < NT:
                        act.dma_start(x_in[:, t % 2, :], x_tiles[:, t + 2, :]).then_inc(x_again[t % 2], 16)
                    square("x2", t, 2 * NT + t)

            act.wait_ge(z_full, 2 * NCH * PAIRS)
            act.dma_start(g_post_t[:, :], g_mix_post.partition_broadcast(P)).then_inc(gain2_in, 16)
            act.dma_start(g_ffn_t[:, :], g_ffn_pre.partition_broadcast(P)).then_inc(gain2_in, 16)
            for t in range(2):
                act.dma_start(x_in[:, t, :], x_tiles[:, t, :]).then_inc(x_again[t], 16)
            split_at(0, [(acc_full, ACC_END - 16)])
            step(PAIRS, 0, proj=False, slots=TAIL_SLOTS)
            for i in range(NORM_IN_TAIL, len(NORM)):
                norm_x2(i - 1)
                norm(i)
                if i in FIRST_SPLITS:
                    m = FIRST_SPLITS[i]
                    split_at(m, [(t_full, T_TRANS) if m == 1 else (acc_full, ACC_END)])
            act.dma_start(g_out[:, :], g_ffn_post.partition_broadcast(P)).then_inc(gain3_in, 16)

            def ffn_chunk(g, e, par, c):
                n = 4 * g + 2 * e + c
                act.wait_ge(up_full, n + 1)
                if not (isinstance(n, int) and n < 2):
                    act.wait_ge(h_ready, n - 1)
                gate_b = FIRST_GATE_B[2 * e + c] if isinstance(g, int) and g == 0 else GATEB[c]
                nc.scalar.activation(sg[:, c, :], gate_b[:, :], ACT.Sigmoid).then_inc(sg_ready, 1)
                act.wait_ge(prod_ready, n + 1)
                nc.scalar.activation(h_hi[:, par, e, c * HALF:(c + 1) * HALF], sg[:, c, :],
                                     ACT.Copy).then_inc(h_hi_ready, 1)

            ffn_chunk(0, 0, 0, 0)
            split_at(3, [(gate_full, 3)])
            ffn_chunk(0, 0, 0, 1)
            split_at(4, [(up_full, 2)])
            for c in range(2):
                ffn_chunk(0, 1, 0, c)

            def ffn_step(g, par, m_mod):
                base = 6 * g - 2

                def split(off, s, count):
                    act.wait_ge(s, count)
                    n = UNITS1 + base + off
                    rp = off % 2
                    rc = 16 * (n // 2 + 1) if isinstance(n, int) else 8 * (n - rp) + 16
                    split_hi(n, ring(m_mod + off), rp, rc)

                split(1, gate_full, 4 * g + 1)
                split(2, gate_full, 4 * g + 1)
                split(3, gate_full, 4 * g + 2)
                ffn_chunk(g, 0, par, 0)
                split(4, up_full, 4 * g + 2)
                ffn_chunk(g, 0, par, 1)
                split(5, gate_full, 4 * g + 4)
                ffn_chunk(g, 1, par, 0)
                split(6, up_full, 4 * g + 4)
                ffn_chunk(g, 1, par, 1)

            with act.Fori(0, (NG - 1) // 2) as i:
                for u in range(2):
                    ffn_step(2 * i + 1 + u, (1 + u) % 2, (4 + 6 * u) % 3)
            act.wait_ge(up_full, 4 * NG)
            split_hi(UNITS - 1, LAST_SLOT, 1, 16 * (UNITS // 2))
            for t in range(NT):
                for c in range(2):
                    act.wait_ge(y_free, 16 * (NG - 1) + 2 * t + c + 1)
                    if t or c:
                        act.wait_ge(ysq_done, 2 * t + c)
                    nc.scalar.activation(sg[:, c, :], y[:, t, c * HALF:(c + 1) * HALF], ACT.Square,
                                         accum_out=ss[:, (2 * t + c):(2 * t + c) + 1]).then_inc(ysq_done, 1)

        @block.gpsimd
        def _(pool):
            nc.gpsimd.memset(ident[:, :], 0.0).then_inc(consts, 1)
            nc.gpsimd.memset(mhalf[:, :], -0.5).then_inc(consts, 1)
            for b in range(2):
                nc.gpsimd.memset(stay[b][:, 0:1], 1.0).then_inc(consts, 1)
            nc.gpsimd.memset(keep[:, :], 1.0).then_inc(consts, 1)
            pool.wait_ge(consts, 5)
            nc.gpsimd.affine_select(out=ident[:, :], in_=ident[:, :], compare_op=ALU.not_equal, fill=1.0,
                                    base=0, pattern=[[-1, P]], channel_multiplier=1).then_inc(consts, 1)
            nc.gpsimd.affine_select(out=keep[:, :], in_=keep[:, :], compare_op=ALU.is_gt, fill=0.0,
                                    base=0, pattern=[[1, P]], channel_multiplier=-1).then_inc(consts, 1)
            pool.wait_ge(consts, 7)

            def split_lo(n, slot, raw_slot):
                pool.wait_ge(w_hi_ready, n + 1)
                nc.gpsimd.tensor_tensor(w_lo[slot], raw[:, raw_slot, :], w_hi[slot].bitcast(F32),
                                        ALU.subtract).then_inc(w_ready, 1)

            def inverse_rms(col, count):
                nc.gpsimd.tensor_scalar(ms[:, col:col + 1], ss[:, col:col + 1], 1.0 / D, EPS,
                                        ALU.mult, ALU.add).then_inc(ms_done, 1)
                pool.wait_ge(ms_done, count + 1)
                nc.gpsimd.tensor_tensor(rstd[:, col:col + 1], ms[:, col:col + 1], mhalf[:, :],
                                        ALU.pow).then_inc(rstd_done, 1)

            for t in range(NT):
                pool.wait_ge(sq_done, t + 1)
                inverse_rms(t, t)
                if t == 3:
                    split_lo(0, 0, 0)
            split_lo(1, 1, 1)
            split_lo(2, 0, 0)

            def step(p, first=False):
                for s in range(SLOTS):
                    if first and 8 <= s < 8 + NT:
                        if s == 8:
                            pool.wait_ge(hn_ready, NT)
                        nc.gpsimd.memset(acc[:, s - 8, :], 0.0)
                    if s in Z_SLOT:
                        h, c = Z_SLOT[s]
                        r, a, _, _ = CHUNKS[c]
                        if a == P * r:
                            pool.wait_ge(sig_done, 2 * NCH * p + NCH * h + c + 1)
                            diag = A[r // 4][:, ROW_AT[r]:ROW_AT[r] + P]
                            nc.gpsimd.tensor_tensor(diag, diag, keep[:, :], ALU.mult)
                            diag = stay[r % 2][:, 1:1 + P]
                            nc.gpsimd.affine_select(out=diag, in_=diag, compare_op=ALU.is_gt, fill=1.0, base=0,
                                                    pattern=[[1, P]], channel_multiplier=-1).then_inc(mask_done, 1)
                    if ROW_SLOT.get(s) in POOL_ROWS:
                        h, r = ROW_SLOT[s]
                        R = 16 * p + 8 * h + r
                        pool.wait_ge(scan_done, R + 1)
                        a = A[r // 4][:, ROW_AT[r]:ROW_AT[r] + ROW_W[r]]
                        nc.gpsimd.tensor_tensor(a, a, stay[r % 2][:, 0:ROW_W[r]], ALU.mult).then_inc(row_done, 1)
                    if s % 8 == 1 and has_unit(p, s):
                        kind = FILL_KIND[s // 8]
                        par = 1 - unit_parity(p, kind)
                        split_lo(step_units(p, kind)[1] + 1, par, par)

            step(0, first=True)
            with pool.Fori(0, PAIRS // 2 - 1) as i:
                for u in range(2):
                    step(2 * i + 1 + u)
            step(PAIRS - 1)
            split_lo(UNITS1, ring(0), 0)
            for i, (add, scale, _, _) in enumerate(NORM):
                if add is not None:
                    pool.wait_ge(sq_done, square_index("mix", add) + 1)
                    inverse_rms(NT + add, square_index("mix", add))
                t = NORM[i - 1][1] if i else None
                if t is not None:
                    pool.wait_ge(sq_done, square_index("x2", t) + 1)
                    inverse_rms(2 * NT + t, square_index("x2", t))
                if scale is not None:
                    t = scale
                    pool.wait_ge(mix_scaled, t + 1)
                    pool.wait_ge(x_again[t % 2], 16 * (t // 2 + 1))
                    nc.gpsimd.tensor_tensor(acc[:, t, :], acc[:, t, :], x_in[:, t % 2, :],
                                            ALU.add).then_inc(x2_ready, 1)
                if i in FIRST_SPLITS:
                    m = FIRST_SPLITS[i]
                    split_lo(UNITS1 + m, ring(m), m % 2)

            def h_lo_chunk(g, e, par, c):
                n = 4 * g + 2 * e + c
                pool.wait_ge(h_hi_ready, n + 1)
                cols = slice(c * HALF, (c + 1) * HALF)
                nc.gpsimd.tensor_tensor(h_lo[:, par, e, cols], sg[:, c, :], h_hi[:, par, e, cols].bitcast(F32),
                                        ALU.subtract).then_inc(h_ready, 1)

            h_lo_chunk(0, 0, 0, 0)
            split_lo(UNITS1 + 3, ring(3), 1)
            h_lo_chunk(0, 0, 0, 1)
            split_lo(UNITS1 + 4, ring(4), 0)
            pool.wait_ge(hn_ready, 2 * NT)
            pool.wait_ge(t_lo, T_END)
            nc.gpsimd.memset(y[:, :, :], 0.0).then_inc(y_zero, 1)
            for c in range(2):
                h_lo_chunk(0, 1, 0, c)
            with pool.Fori(0, (NG - 1) // 2) as i:
                for u in range(2):
                    g, par, m_mod = 2 * i + 1 + u, (1 + u) % 2, (4 + 6 * u) % 3
                    base = UNITS1 + 6 * g - 2
                    for off in (1, 2, 3):
                        split_lo(base + off, ring(m_mod + off), off % 2)
                    for off in (4, 5, 6, None):
                        e, c = (0, 0) if off == 4 else (0, 1) if off == 5 else (1, 0) if off == 6 else (1, 1)
                        h_lo_chunk(g, e, par, c)
                        if off:
                            split_lo(base + off, ring(m_mod + off), off % 2)
            split_lo(UNITS - 1, LAST_SLOT, 1)
            for t in range(NT):
                pool.wait_ge(ysq_done, 2 * t + 2)
                nc.gpsimd.tensor_tensor(ss[:, 3 * NT + t:3 * NT + t + 1], ss[:, 2 * t:2 * t + 1],
                                        ss[:, 2 * t + 1:2 * t + 2], ALU.add).then_inc(ms_done, 1)
                pool.wait_ge(ms_done, 3 * NT + 2 * t + 1)
                nc.gpsimd.tensor_scalar(ms[:, t:t + 1], ss[:, 3 * NT + t:3 * NT + t + 1], 1.0 / D, EPS,
                                        ALU.mult, ALU.add).then_inc(ms_done, 1)
                pool.wait_ge(ms_done, 3 * NT + 2 * t + 2)
                nc.gpsimd.tensor_tensor(rstd[:, t:t + 1], ms[:, t:t + 1], mhalf[:, :],
                                        ALU.pow).then_inc(rstd_done, 1)
                if t % 2:
                    pool.wait_ge(y_scaled, t)
                    nc.gpsimd.tensor_tensor(y[:, t - 1, :], y[:, t - 1, :], acc[:, t - 1, :],
                                            ALU.add).then_inc(even_out, 1)

        @block.vector
        def _(dve):
            def t_lo_sub(index, out_ap, in_ap, hi_ap):
                dve.wait_ge(t_hi, index + 1)
                nc.vector.tensor_tensor(out_ap, in_ap, hi_ap.bitcast(F32), ALU.subtract).then_inc(t_lo, 1)

            def norm_lo(index, t, half):
                ks, cols = slice(4 * half, 4 * half + 4), slice(t * P, (t + 1) * P)
                t_lo_sub(index, hnT_lo[:, ks, cols], TB[index % 2][:, :].rearrange("p (k c) -> p k c", k=4),
                         hnT_hi[:, ks, cols])

            dve.wait_ge(gain_in, 16)
            for t in range(NT + 1):
                if t < NT:
                    dve.wait_ge(rstd_done, t + 1)
                    if t >= 2:
                        dve.wait_ge(t_full, 2 * (t - 1))
                    nc.vector.scalar_tensor_tensor(out=hn_s[:, t % 2, :], in0=acc[:, t, :],
                                                   scalar=rstd[:, t:t + 1], in1=g_pre_s[:, :],
                                                   op0=ALU.mult, op1=ALU.mult).then_inc(hn_ready, 1)
                if t:
                    norm_lo(2 * t - 2, t - 1, 0)
                    norm_lo(2 * t - 1, t - 1, 1)

            def qk_lo(hi_count, kind, par, c, src):
                dve.wait_ge(acc_hi, hi_count)
                cols = slice(c * HALF, (c + 1) * HALF)
                for h in range(2):
                    hi = q_hi2[OWN[h], h, cols] if kind == "q" else k_tile(h, par)[OWN[h], cols]
                    lo = q_lo[OWN[h], cols] if kind == "q" else k_tile(h, par)[OTHER[h], cols]
                    sub = nc.vector.tensor_tensor(lo, src[OWN[h], :], hi.bitcast(F32), ALU.subtract)
                sub.then_inc(acc_free, 1)

            for n, (kind, c) in enumerate(FIRST_ACC):
                qk_lo(n + 1, kind, 0, c, FIRST_ACC_B[n])
            def out_add(index, t, c):
                dve.wait_ge(acc_full, index + 1)
                cols = slice(c * HALF, (c + 1) * HALF)
                nc.vector.tensor_tensor(acc[:, t, cols], ACCB[c][:, :], acc[:, t, cols],
                                        ALU.add).then_inc(acc_free, 1)

            def o_add(p, dp, h, half_q, half):
                dve.wait_ge(o_half, 8 * (p + dp) + 4 * h + 2 * half_q + half + 1)
                nc.vector.tensor_tensor(o_part[OWN[h], half, :], OB[half_q][0:HD, half * 256:half * 256 + 256],
                                        o_part[OWN[h], half, :], ALU.add).then_inc(o_sum, 1)

            def o_lo_sub(p, dp, h, half_q, half):
                dve.wait_ge(o_hi, 8 * (p + dp) + 4 * h + 2 * half_q + half + 1)
                cols = slice(HALF * half_q + 256 * half, HALF * half_q + 256 * half + 256)
                nc.vector.tensor_tensor(oT_lo[OWN[h], cols], o_part[OWN[h], half, :],
                                        oT_hi[OWN[h], cols].bitcast(F32), ALU.subtract).then_inc(o_lo, 1)

            def projections(p, par, s, first, proj):
                if s == 0 and not first:
                    qk_lo(4 * p + 4, "q", par, 1, ACCB[1])
                if proj and s in (20, 24):
                    qk_lo(4 * p + 4 + s // 24 + 1, "k", 1 - par, s // 24, ACCB[s // 24])
                if proj and s == 28:
                    qk_lo(4 * p + 4 + 3, "q", 1 - par, 0, ACCB[0])

            def step(p, par, first=False, proj=True, wo=True, slots=SLOTS):
                tail = slots < SLOTS
                for s in range(slots):
                    if not tail and wo and 8 <= s <= 16:
                        index = step_units(p, "wo")[0]
                        if s == 8:
                            dve.wait_ge(acc_free, index)
                        if s > 8:
                            out_add(index + 2 * (s - 9) + 1, s - 9, 1)
                        if s < 16:
                            out_add(index + 2 * (s - 8), s - 8, 0)
                    row = ROW_SLOT.get(s) if not tail else None
                    if row:
                        h, r = row
                        R = 16 * p + 8 * h + r
                        row_w, st = ROW_W[r], stay[r % 2]
                        dve.wait_ge(mask_done, R + 1)
                        dve.wait_ge(sig_done, 2 * NCH * p + NCH * h + LAST_CHUNK[r] + 1)
                        live = st[:, 1:1 + row_w]
                        nc.vector.tensor_tensor_scan(live, live, live, 1.0, ALU.mult,
                                                     ALU.bypass).then_inc(scan_done, 1)
                    for n, kind, h, j in T_SLOT.get(s, []):
                        g = t_index(p, n)
                        b = n % 2
                        if kind == "v" and not tail:
                            t_lo_sub(g, V[:, j:j + 4, :, 1, :],
                                     TB[b][:, :].rearrange("p (k h c) -> p k h c", k=4, h=2),
                                     V[:, j:j + 4, :, 0, :])
                        elif kind != "v" and not (kind == "prev" and first):
                            w = P * (min(j, 3) + 1 if kind == "lo" else j - 3)
                            t_lo_sub(g, AT_lo[:, b, 0:w], TB[b][:, 0:w], AT_hi[:, b, 0:w])
                    if not tail:
                        projections(p, par, s, first, proj)
                    if row and row not in POOL_ROWS:
                        if row == AFTER_POOL_ROWS:
                            dve.wait_ge(row_done, R)
                        dve.wait_ge(scan_done, R + 1)
                        a = A[row[1] // 4][:, ROW_AT[row[1]]:ROW_AT[row[1]] + row_w]
                        nc.vector.tensor_tensor(a, a, st[:, 0:row_w], ALU.mult).then_inc(row_done, 1)
                    if not tail:
                        for o in value_halves(s - 1, first, tail):
                            o_lo_sub(p, *o)
                    for o in value_halves(s, first, tail):
                        o_add(p, *o)
                    if tail and s >= TAIL:
                        norm(s - TAIL)
                    if tail:
                        for o in value_halves(s, first, tail):
                            o_lo_sub(p, *o)

            step(0, 0, first=True, wo=False)
            with dve.Fori(0, PAIRS // 2 - 1) as i:
                for u in range(2):
                    step(2 * i + 1 + u, (1 + u) % 2)
            step(PAIRS - 1, 1, proj=False)

            def norm(i):
                add, scale, normed, split = NORM[i]
                if i == 0:
                    dve.wait_ge(acc_free, ACC_END - 16)
                if add is not None:
                    for c in range(2):
                        out_add(ACC_END - 16 + 2 * add + c, add, c)
                if scale is not None:
                    t = scale
                    if t == 0:
                        dve.wait_ge(gain2_in, 32)
                    dve.wait_ge(rstd_done, square_index("mix", t) + 1)
                    nc.vector.scalar_tensor_tensor(out=acc[:, t, :], in0=acc[:, t, :],
                                                   scalar=rstd[:, NT + t:NT + t + 1], in1=g_post_t[:, :],
                                                   op0=ALU.mult, op1=ALU.mult).then_inc(mix_scaled, 1)
                if normed is not None:
                    t = normed
                    dve.wait_ge(rstd_done, square_index("x2", t) + 1)
                    if t >= 2:
                        dve.wait_ge(t_full, T_TRANS + 2 * (t - 1))
                    nc.vector.scalar_tensor_tensor(out=hn_t[:, t % 2, :], in0=acc[:, t, :],
                                                   scalar=rstd[:, 2 * NT + t:2 * NT + t + 1],
                                                   in1=g_ffn_t[:, :], op0=ALU.mult,
                                                   op1=ALU.mult).then_inc(hn_ready, 1)
                if split is not None:
                    for half in range(2):
                        norm_lo(T_TRANS + 2 * split + half, split, half)

            step(PAIRS, 0, proj=False, wo=False, slots=TAIL_SLOTS)
            for i in range(NORM_IN_TAIL, len(NORM)):
                norm(i)

            def ffn_chunk(g, e, par, c):
                n = 4 * g + 2 * e + c
                dve.wait_ge(sg_ready, n + 1)
                gate_b = FIRST_GATE_B[2 * e + c] if isinstance(g, int) and g == 0 else GATEB[c]
                nc.vector.tensor_tensor(sg[:, c, :], gate_b[:, :], sg[:, c, :], ALU.mult).then_inc(silu_ready, 1)
                dve.wait_ge(silu_ready, n + 1)
                nc.vector.tensor_tensor(sg[:, c, :], UPB[c][:, :], sg[:, c, :], ALU.mult).then_inc(prod_ready, 1)

            for e in range(2):
                for c in range(2):
                    ffn_chunk(0, e, 0, c)
            dve.wait_ge(y_zero, 1)

            def y_add(g, k):
                n = 16 * g + k
                dve.wait_ge(y_full, n + 1)
                cols = slice((k % 2) * HALF, (k % 2 + 1) * HALF)
                nc.vector.tensor_tensor(y[:, k // 2, cols], YB[k % 4][:, :], y[:, k // 2, cols],
                                        ALU.add).then_inc(y_free, 1)

            with dve.Fori(0, (NG - 1) // 2) as i:
                for u in range(2):
                    g, par = 2 * i + 1 + u, (1 + u) % 2
                    for c in range(2):
                        ffn_chunk(g, 0, par, c)
                    for c in range(2):
                        ffn_chunk(g, 1, par, c)
                    dve.wait_ge(prod_ready, 4 * g + 4)
                    for k in range(16):
                        y_add(g - 1, k)

            dve.wait_ge(y_free, 16 * (NG - 1))
            dve.wait_ge(gain3_in, 16)

            def scale_out(t, cols):
                dve.wait_ge(rstd_done, 3 * NT + t + 1)
                nc.vector.scalar_tensor_tensor(out=y[:, t, cols], in0=y[:, t, cols], scalar=rstd[:, t:t + 1],
                                               in1=g_out[:, cols], op0=ALU.mult, op1=ALU.mult).then_inc(y_scaled, 1)

            def add_out(t, cols, count):
                dve.wait_ge(y_scaled, count)
                nc.vector.tensor_tensor(y[:, t, cols], y[:, t, cols], acc[:, t, cols],
                                        ALU.add).then_inc(odd_out, 1)

            for t in range(NT):
                y_add(NG - 1, 2 * t)
                y_add(NG - 1, 2 * t + 1)
                if t:
                    scale_out(t - 1, slice(0, D))
                if t > 1 and t % 2 == 1:
                    add_out(t - 2, slice(0, D), t - 1)
            for c in range(2):
                cols = slice(c * HALF, (c + 1) * HALF)
                scale_out(NT - 1, cols)
                add_out(NT - 1, cols, NT + c)

        @block.tensor
        def _(pe):
            def project_tiles(c, slot, kts, dst):
                for kt in kts:
                    wh = w_hi[slot][:, kt * P:(kt + 1) * P]
                    wl = w_lo[slot][:, kt * P:(kt + 1) * P]
                    cols = slice(c * HALF, (c + 1) * HALF)
                    nc.tensor.matmul(dst[:, :], wh, hnT_hi[:, kt, cols], start=(kt == 0), stop=False)
                    nc.tensor.matmul(dst[:, :], wh, hnT_lo[:, kt, cols], start=False, stop=False)
                    mm = nc.tensor.matmul(dst[:, :], wl, hnT_hi[:, kt, cols], start=False, stop=(kt == KT - 1))
                if kts[-1] == KT - 1:
                    mm.then_inc(acc_full, 1)

            def transpose_norm(n, src, half):
                if n >= 2:
                    pe.wait_ge(t_lo, n - 1)
                for q in range(4):
                    k = 4 * half + q
                    mm = nc.tensor.transpose(TB[n % 2][:, q * P:(q + 1) * P], src[:, k * P:(k + 1) * P], ident[:, :])
                mm.then_inc(t_full, 1)

            pe.wait_ge(consts, 7)
            for t in range(NT + 1):
                if t < NT:
                    pe.wait_ge(hn_ready, t + 1)
                    for half in range(2):
                        transpose_norm(2 * t + half, hn_s[:, t % 2, :], half)
                for n, kts in FIRST_PARTS.get(t, []):
                    kind, c = FIRST_ACC[n]
                    unit = "kq".index(kind)
                    pe.wait_ge(w_ready, unit + 1)
                    pe.wait_ge(t_lo, NT * (c + 1))
                    project_tiles(c, unit, kts, FIRST_ACC_B[n])

            def out_project(index, t, c, slot):
                pe.wait_ge(acc_free, index + c - 1)
                cols = slice(c * HALF, (c + 1) * HALF)
                oh, ol = oT_hi[:, t * P:(t + 1) * P], oT_lo[:, t * P:(t + 1) * P]
                nc.tensor.matmul(ACCB[c][:, :], oh, w_hi[slot][:, cols], start=True, stop=False)
                nc.tensor.matmul(ACCB[c][:, :], oh, w_lo[slot][:, cols], start=False, stop=False)
                nc.tensor.matmul(ACCB[c][:, :], ol, w_hi[slot][:, cols], start=False, stop=True
                                 ).then_inc(acc_full, 1)

            def out_last(k, c):
                if k == 0 and c == 0:
                    pe.wait_ge(w_ready, UNITS1)
                    pe.wait_ge(o_lo, 8 * PAIRS - 2)
                if k == 4 and c == 0:
                    pe.wait_ge(o_lo, 8 * PAIRS)
                out_project(ACC_END - 16 + 2 * k, k, c, 1)

            def fill(p, s, part, proj, wo):
                kind = FILL_KIND[s // 8]
                if kind == "wo":
                    if wo:
                        index, n = step_units(p, "wo")
                        if s == 8 and part == 0:
                            pe.wait_ge(w_ready, n + 1)
                            pe.wait_ge(o_lo, 8 * p - 2)
                        if s == 12 and part == 0:
                            pe.wait_ge(o_lo, 8 * p)
                        out_project(index + 2 * (s - 8), s - 8, part, unit_parity(p, "wo"))
                elif proj or kind == "v":
                    index, n = step_units(p, kind)
                    c = (s % 8) // 4
                    if part == 0:
                        if s % 8 == 0:
                            pe.wait_ge(w_ready, n + 1)
                        if s % 4 == 0:
                            pe.wait_ge(acc_free, index + c - 1)
                    k0 = 2 * (s % 4) + part
                    project_tiles(c, unit_parity(p, kind), range(k0, k0 + 1), ACCB[c])

            def step(p, par, first=False, proj=True, wo=True, slots=SLOTS):
                tail = slots < SLOTS
                for s in range(slots):
                    dp = 0
                    at = s - AV_LAG
                    if at < 0:
                        dp, at = -1, at + SLOTS
                    for n, kind, h, j in T_SLOT.get(at, []):
                        if kind == "v" or first and (dp < 0 or kind == "prev"):
                            continue
                        half_q = 0 if kind == "lo" else 1
                        start = j == (0 if kind == "lo" else 4)
                        stop = j == NT - 1
                        w = P * (min(j, 3) + 1 if kind == "lo" else j - 3)
                        b = n % 2
                        if start:
                            sb = 4 * (p + dp) + 2 * h + half_q - (4 if kind == "prev" else 0)
                            if not (isinstance(sb, int) and sb < 2):
                                pe.wait_ge(o_sum, 2 * (sb - 1))
                        pe.wait_ge(t_lo, t_index(p + dp, n) + 1)
                        v = V[:, j, h, :, :].rearrange("p a c -> p (a c)")
                        nc.tensor.matmul(OB[half_q][:, 0:w], v, AT_hi[:, b, 0:w], start=start, stop=False,
                                         skip_group_check=True)
                        nc.tensor.matmul(OB[half_q][:, 0:w], v, AT_lo[:, b, 0:w], start=False, stop=stop,
                                         skip_group_check=True).then_inc(av_done, 1)
                    if not tail:
                        fill(p, s, 0, proj, wo)
                    elif s >= TAIL and NORM[s - TAIL][0] is not None:
                        out_last(NORM[s - TAIL][0], 0)
                    for n, kind, h, j in T_SLOT.get(s, []):
                        g = t_index(p, n)
                        b = n % 2
                        if kind == "v" and not tail:
                            pe.wait_ge(t_lo, g - 1)
                            pe.wait_ge(acc_free, acc_base(p) + 1 + j // 4)
                            for q in range(4):
                                mm = nc.tensor.transpose(TB[b][:, q * P:(q + 1) * P],
                                                         vT[:, (j + q) * P:(j + q + 1) * P], ident[:, :])
                            mm.then_inc(t_full, 1)
                        elif kind != "v" and not (kind == "prev" and first):
                            pe.wait_ge(t_lo, g - 1)
                            rows = range(0, min(j, 3) + 1) if kind == "lo" else range(4, j + 1)
                            hp = 16 * p + 8 * h - (16 if kind == "prev" else 0)
                            pe.wait_ge(row_done, hp + rows[-1] + 1)
                            for q, r in enumerate(rows):
                                at_ = ROW_AT[r] + (j - r) * P
                                mm = nc.tensor.transpose(TB[b][:, q * P:(q + 1) * P],
                                                         A[r // 4][:, at_:at_ + P], ident[:, :])
                            mm.then_inc(t_full, 1)
                    if s in Z_SLOT and not tail:
                        h, c = Z_SLOT[s]
                        r, a, e, _ = CHUNKS[c]
                        z = 2 * NCH * p + NCH * h + c
                        if s == 0:
                            pe.wait_ge(acc_free, acc_base(p) - 1)
                        if s == 8:
                            pe.wait_ge(acc_free, acc_base(p))
                        if not (isinstance(z, int) and z < 2):
                            pe.wait_ge(sig_done, z - 1)
                        qs, kk = slice(r * P, (r + 1) * P), k_tile(h, par)
                        dst = ZB[c % 2][:, 0:e - a]
                        nc.tensor.matmul(dst, q_hi2[:, h, qs], kk[:, a:e], start=True, stop=False)
                        nc.tensor.matmul(dst, q_lo[OWN[h], qs], kk[OWN[h], a:e], start=False, stop=True
                                         ).then_inc(z_full, 1)
                    if not tail:
                        fill(p, s, 1, proj, wo)
                    elif s >= TAIL and NORM[s - TAIL][0] is not None:
                        out_last(NORM[s - TAIL][0], 1)

            step(0, 0, first=True, wo=False)
            with pe.Fori(0, PAIRS // 2 - 1) as i:
                for u in range(2):
                    step(2 * i + 1 + u, (1 + u) % 2)
            step(PAIRS - 1, 1, proj=False)
            step(PAIRS, 0, proj=False, wo=False, slots=TAIL_SLOTS)

            def gate_up(is_up, c, slot, bank_ap):
                cols = slice(c * HALF, (c + 1) * HALF)
                for kt in range(KT):
                    wh = w_hi[slot][:, kt * P:(kt + 1) * P]
                    wl = w_lo[slot][:, kt * P:(kt + 1) * P]
                    nc.tensor.matmul(bank_ap, wh, hnT_hi[:, kt, cols], start=(kt == 0), stop=False)
                    nc.tensor.matmul(bank_ap, wh, hnT_lo[:, kt, cols], start=False, stop=False)
                    mm = nc.tensor.matmul(bank_ap, wl, hnT_hi[:, kt, cols], start=False, stop=(kt == KT - 1))
                mm.then_inc(up_full if is_up else gate_full, 1)

            def gate_up_first(m, c):
                pe.wait_ge(w_ready, UNITS1 + m + 1)
                if m % 2 == 0:
                    dst = FIRST_GATE_B[m + c]
                else:
                    dst = UPB[c]
                    if m == 3:
                        pe.wait_ge(prod_ready, c + 1)
                gate_up(m % 2 == 1, c, ring(m), dst[:, :])

            for i in range(NORM_IN_TAIL - 1, len(NORM) - 1):
                add, t = NORM[i + 1][0], NORM[i][2]
                if add is not None:
                    for c in range(2):
                        out_last(add, c)
                if t is not None:
                    pe.wait_ge(hn_ready, NT + t + 1)
                    for half in range(2):
                        transpose_norm(T_TRANS + 2 * t + half, hn_t[:, t % 2, :], half)
                if i in FIRST_CHUNKS:
                    pe.wait_ge(t_lo, T_TRANS + NT)
                    gate_up_first(FIRST_CHUNKS[i], 0)

            def down(g, par, slots, last=False):
                pe.wait_ge(h_ready, 4 * g + 4)
                for k in range(16):
                    t, c = k // 2, k % 2
                    cols = slice(c * HALF, (c + 1) * HALF)
                    if k >= 4 or last:
                        pe.wait_ge(y_free, 16 * g + k - 3)
                    for e in range(2):
                        hh = h_hi[:, par, e, t * P:(t + 1) * P]
                        hl = h_lo[:, par, e, t * P:(t + 1) * P]
                        wh, wl = w_hi[slots[e]][:, cols], w_lo[slots[e]][:, cols]
                        nc.tensor.matmul(YB[k % 4][:, :], hh, wh, start=(e == 0), stop=False)
                        nc.tensor.matmul(YB[k % 4][:, :], hh, wl, start=False, stop=False)
                        mm = nc.tensor.matmul(YB[k % 4][:, :], hl, wh, start=False, stop=(e == 1))
                    mm.then_inc(y_full, 1)

            pe.wait_ge(t_lo, T_END)
            for m, c in ((0, 1), (1, 1), (2, 1), (3, 0), (3, 1)):
                gate_up_first(m, c)

            with pe.Fori(0, (NG - 1) // 2) as i:
                for u in range(2):
                    g, par, m_mod = 2 * i + 1 + u, (1 + u) % 2, (4 + 6 * u) % 3
                    base = UNITS1 + 6 * g - 2
                    for m in range(4):
                        pe.wait_ge(w_ready, base + m + 1)
                        for c in range(2):
                            n = 4 * g + 2 * (m // 2) + c
                            if m % 2 == 0:
                                pe.wait_ge(prod_ready, n - 1)
                            gate_up(m % 2 == 1, c, ring(m_mod + m), (UPB if m % 2 else GATEB)[c][:, :])
                    pe.wait_ge(w_ready, base + 6)
                    down(g - 1, 1 - par, [ring(m_mod + 4), ring(m_mod + 5)])
            pe.wait_ge(w_ready, UNITS)
            down(NG - 1, (NG - 1) % 2, [ring(6 * NG - 2), LAST_SLOT], last=True)


def kernel(**inputs):
    import numpy as _np
    import concourse.bacc as _bacc
    from concourse import mybir as _mybir
    from concourse.bass_utils import run_bass_kernel_spmd as _run

    a = {k: _np.asarray(v) for k, v in inputs.items()}

    def col_units(w, n):
        return w[:, n * P:(n + 1) * P].reshape(KT, P, P).transpose(1, 0, 2).reshape(P, D)

    w_qkv, w_o, w_gu, w_down = a["sb_w_qkv"][0], a["sb_w_o"][0], a["ffn_w_gu"][0], a["ffn_w_down"][0]
    q = [col_units(w_qkv, p) for p in range(PAIRS)]
    k = [col_units(w_qkv, PAIRS + p) for p in range(PAIRS)]
    v = [col_units(w_qkv, 2 * PAIRS + p) for p in range(PAIRS)]
    wo = [w_o[p * P:(p + 1) * P] for p in range(PAIRS)]
    gate = [col_units(w_gu, f) for f in range(NF)]
    up = [col_units(w_gu, NF + f) for f in range(NF)]
    down = [w_down[f * P:(f + 1) * P] for f in range(NF)]
    order = [k[0], q[0], v[0], k[1], q[1]]
    for p in range(1, PAIRS - 1):
        order += [v[p], wo[p - 1], k[p + 1], q[p + 1]]
    order += [v[PAIRS - 1], wo[PAIRS - 2], wo[PAIRS - 1], gate[0], up[0], gate[1], up[1]]
    for g in range(1, NG):
        order += [gate[2 * g], up[2 * g], gate[2 * g + 1], up[2 * g + 1], down[2 * g - 2], down[2 * g - 1]]
    order += [down[NF - 2], down[NF - 1]]

    arrays = {
        "in_x": _np.ascontiguousarray(a["x"][:, ::-1]),
        "in_mix_pre": _np.ascontiguousarray(a["ln_mix_pre"][0]),
        "in_mix_post": _np.ascontiguousarray(a["ln_mix_post"][0]),
        "in_ffn_pre": _np.ascontiguousarray(a["ln_ffn_pre"][0]),
        "in_ffn_post": _np.ascontiguousarray(a["ln_ffn_post"][0]),
        "in_units": _np.ascontiguousarray(_np.stack(order)),
    }
    nc = _bacc.Bacc("TRN2", target_bir_lowering=False, num_devices=1)
    args = [nc.dram_tensor(n, t.shape, _mybir.dt.from_np(t.dtype), kind="ExternalInput").ap()
            for n, t in arrays.items()]
    args.append(nc.dram_tensor("out_0", a["x"].shape, _mybir.dt.float32, kind="ExternalOutput").ap())
    encoder_layer(nc, *args)
    r = _run(nc, [arrays], core_ids=[0])
    return _np.ascontiguousarray(_np.asarray(r.results[0]["out_0"])[:, ::-1])
```
